# Optimizing a Trainium2 kernel written in Bass

```python
import math
import jax
import jax.numpy as jnp
from jax import lax
import numpy as np

D_MODEL = 2048
BATCH = 1
SEQ = 256
DEPTH = 2

CTX_LEN = 256
GRID_W = 64
N_EVEN = (DEPTH + 1) // 2
N_ODD = DEPTH // 2
ADA_CHUNKS = 6
NORM_EPS = 1e-6

A_WIDTH = D_MODEL // 2
A_HEAD_DIM = 64
A_HEADS = A_WIDTH // (2 * A_HEAD_DIM)
ROPE_BASE = 10000.0
Q_BLOCK = 128

B_WIDTH = D_MODEL - A_WIDTH
B_HEAD_DIM = 64
B_HEADS = B_WIDTH // B_HEAD_DIM
DECAY_LORA = 64
ICLR_LORA = 64
GATE_LORA = 160
GN_EPS = 64e-5
B_COLS = 3 * B_WIDTH + 2 * DECAY_LORA + 2 * ICLR_LORA + GATE_LORA
IN_COLS = 3 * A_WIDTH + B_COLS

CONV_WIDTH = 31
CONV_CH = D_MODEL

D_FF = 4 * D_MODEL

kernel_name = 'hybrid_diffattn_rwkv7_conformer_dit'

def rms_norm(x, g):
    xf = x.astype(jnp.float32)
    y = xf * lax.rsqrt(jnp.mean(xf * xf, axis=-1, keepdims=True) + NORM_EPS)
    return (y * g.astype(jnp.float32)).astype(x.dtype)

def modulate(xn, shift, scale):
    return xn * (1 + scale) + shift

def squared_relu_mlp(h, w1, w2):
    return jnp.square(jax.nn.relu(h @ w1)) @ w2

def axial_rope_tables(n_tokens):
    rows = n_tokens // GRID_W
    row_pos = jnp.repeat(jnp.arange(rows, dtype=jnp.float32), GRID_W)
    col_pos = jnp.tile(jnp.arange(GRID_W, dtype=jnp.float32), rows)
    n_freq = A_HEAD_DIM // 4
    inv_freq = ROPE_BASE ** (-jnp.arange(n_freq, dtype=jnp.float32) / n_freq)
    ang = jnp.stack([row_pos[:, None] * inv_freq, col_pos[:, None] * inv_freq], axis=1)
    ang = jnp.stack([ang, ang], axis=2)
    return jnp.cos(ang), jnp.sin(ang)

def apply_axial_rope(x, cos, sin):
    shp = x.shape
    xr = x.astype(jnp.float32).reshape(shp[:-1] + (2, 2, shp[-1] // 4))
    rot = jnp.stack([-xr[..., 1, :], xr[..., 0, :]], axis=-2)
    out = xr * cos[:, None, None] + rot * sin[:, None, None]
    return out.reshape(shp).astype(x.dtype)

def diff_attend(q, k, v, lam):
    s = jnp.einsum('bqhmd,bkhmd->bhmqk', q, k, preferred_element_type=jnp.float32) * (A_HEAD_DIM ** -0.5)
    p = jax.nn.softmax(s, axis=-1)
    p_diff = p[:, :, 0] - lam * p[:, :, 1]
    return jnp.einsum('bhqk,bkhe->bqhe', p_diff.astype(v.dtype), v)

def diff_attention(a_lat, a_ctx, ap, lam_init, cos, sin, need_ctx_out):
    def heads_qk(t, g):
        return rms_norm(t.reshape(t.shape[:2] + (A_HEADS, 2, A_HEAD_DIM)), g)

    def heads_v(t):
        return t.reshape(t.shape[:2] + (A_HEADS, 2 * A_HEAD_DIM))

    q_l, k_l, v_l = jnp.split(a_lat, 3, axis=-1)
    q_c, k_c, v_c = jnp.split(a_ctx, 3, axis=-1)
    q_l = apply_axial_rope(heads_qk(q_l, ap['q_norm']), cos, sin)
    k_l = apply_axial_rope(heads_qk(k_l, ap['k_norm']), cos, sin)
    k_c = heads_qk(k_c, ap['k_norm'])
    v_c = heads_v(v_c)
    k_all = jnp.concatenate([k_c, k_l], axis=1)
    v_all = jnp.concatenate([v_c, heads_v(v_l)], axis=1)
    f32 = jnp.float32
    lam = (jnp.exp(jnp.sum(ap['lq1'].astype(f32) * ap['lk1'].astype(f32)))
           - jnp.exp(jnp.sum(ap['lq2'].astype(f32) * ap['lk2'].astype(f32))) + lam_init)
    bsz, n = q_l.shape[:2]
    nb = n // Q_BLOCK
    q_blocks = jnp.moveaxis(q_l.reshape((bsz, nb, Q_BLOCK) + q_l.shape[2:]), 1, 0)
    o_l = lax.map(lambda qb: diff_attend(qb, k_all, v_all, lam), q_blocks)
    o_l = jnp.moveaxis(o_l, 0, 1).reshape((bsz, n, A_HEADS, 2 * A_HEAD_DIM))

    def finish(o):
        return (rms_norm(o, ap['subln']) * (1 - lam_init)).reshape(o.shape[:2] + (A_WIDTH,))

    y_ctx = finish(diff_attend(heads_qk(q_c, ap['q_norm']), k_c, v_c, lam)) if need_ctx_out else None
    return finish(o_l), y_ctx

def bidir_token_shift(p, mu):
    pad = jnp.pad(p, ((0, 0), (1, 1), (0, 0)))
    nb = 0.5 * (pad[:, :-2] + pad[:, 2:])
    return p + mu * (nb - p)

def rwkv7_inputs(bs, rw):
    bs = bs.astype(jnp.float32)
    cuts = [int(v) for v in np.cumsum([B_WIDTH] * 3 + [DECAY_LORA] * 2 + [ICLR_LORA] * 2)]
    r, k, v, wl_f, wl_b, al_f, al_b, glo = jnp.split(bs, cuts, axis=-1)

    def hd(t):
        return t.reshape(t.shape[:-1] + (B_HEADS, B_HEAD_DIM))

    kk = hd(k * rw['k_k'])
    kk = kk / jnp.maximum(jnp.sqrt(jnp.sum(kk * kk, axis=-1, keepdims=True)), 1e-12)
    decays, keys, iclrs = [], [], []
    for d, (wl, al) in enumerate(((wl_f, al_f), (wl_b, al_b))):
        w_log = -jax.nn.softplus(-(rw['w0'][d] + jnp.tanh(wl) @ rw['w_up'][d])) - 0.5
        a = jax.nn.sigmoid(rw['a0'][d] + al @ rw['a_up'][d])
        decays.append(hd(jnp.exp(-jnp.exp(w_log))))
        keys.append(hd(k * (1 + (a - 1) * rw['k_a'])))
        iclrs.append(hd(a))
    return {'r': hd(r), 'v': hd(v), 'kk': kk, 'decay': decays, 'k': keys, 'a': iclrs, 'glo': glo}

def rwkv7_scan(r, decay, k, v, kk, a, state0, emit):
    def step(S, inp):
        w_t, k_t, v_t, kk_t, a_t = inp[:5]
        S = (S * w_t[:, :, None, :]
             - jnp.einsum('bhvk,bhk->bhv', S, kk_t)[..., None] * (kk_t * a_t)[:, :, None, :]
             + v_t[..., None] * k_t[:, :, None, :])
        return S, (jnp.einsum('bhvk,bhk->bhv', S, inp[5]) if emit else None)

    seqs = (decay, k, v, kk, a) + ((r,) if emit else ())
    xs = tuple(jnp.moveaxis(t, 1, 0) for t in seqs)
    S, o = lax.scan(step, state0, xs)
    return S, (jnp.moveaxis(o, 0, 1) if emit else None)

def rwkv7_readout(o, s, rw):
    mu = jnp.mean(o, axis=-1, keepdims=True)
    var = jnp.mean(jnp.square(o - mu), axis=-1, keepdims=True)
    y = ((o - mu) * lax.rsqrt(var + GN_EPS) * rw['gn_w'].reshape(B_HEADS, B_HEAD_DIM)
         + rw['gn_b'].reshape(B_HEADS, B_HEAD_DIM))
    bonus = sum(jnp.sum(s['r'] * kd * rw['r_k'], axis=-1, keepdims=True) for kd in s['k']) * s['v']
    y = y + bonus
    g = jax.nn.sigmoid(s['glo']) @ rw['g_up']
    return y.reshape(y.shape[:2] + (B_WIDTH,)) * g

def rwkv7_mixer(b_lat, b_ctx, rw, need_ctx_out):
    lat = rwkv7_inputs(bidir_token_shift(b_lat, rw['mu']), rw)
    ctx = rwkv7_inputs(bidir_token_shift(b_ctx, rw['mu']), rw)
    S0 = jnp.zeros((b_lat.shape[0], B_HEADS, B_HEAD_DIM, B_HEAD_DIM), jnp.float32)
    o_lat, o_ctx = 0.0, 0.0
    for d in range(2):
        def rev(t, d=d):
            return jnp.flip(t, axis=1) if d else t

        def seq(s, d=d):
            return [rev(t) for t in (s['r'], s['decay'][d], s['k'][d], s['v'], s['kk'], s['a'][d])]

        S_c, o_c = rwkv7_scan(*seq(ctx), S0, emit=need_ctx_out)
        _, o_l = rwkv7_scan(*seq(lat), S_c, emit=True)
        o_lat = o_lat + rev(o_l)
        if need_ctx_out:
            o_ctx = o_ctx + rev(o_c)
    y_lat = rwkv7_readout(o_lat, lat, rw).astype(b_lat.dtype)
    y_ctx = rwkv7_readout(o_ctx, ctx, rw).astype(b_ctx.dtype) if need_ctx_out else None
    return y_lat, y_ctx

def even_mixer(hn_lat, hn_ctx, w_in, w_out, ap, rw, lam_init, cos, sin, need_ctx_out):
    p_lat = hn_lat @ w_in
    p_ctx = hn_ctx @ w_in
    att_lat, att_ctx = diff_attention(p_lat[..., :3 * A_WIDTH], p_ctx[..., :3 * A_WIDTH], ap, lam_init, cos, sin, need_ctx_out)
    rw_lat, rw_ctx = rwkv7_mixer(p_lat[..., 3 * A_WIDTH:], p_ctx[..., 3 * A_WIDTH:], rw, need_ctx_out)
    y_lat = jnp.concatenate([att_lat, rw_lat], axis=-1) @ w_out
    y_ctx = (jnp.concatenate([att_ctx, rw_ctx], axis=-1) @ w_out) if need_ctx_out else None
    return y_lat, y_ctx

def conformer_conv(h, pw1_w, pw1_b, dw_w, dw_b, ln_g, ln_b, pw2_w, pw2_b):
    u = h @ pw1_w + pw1_b
    u = u[..., :CONV_CH] * jax.nn.sigmoid(u[..., CONV_CH:])
    u = lax.conv_general_dilated(u, dw_w[:, None, :].astype(u.dtype), window_strides=(1,),
                                 padding=[(CONV_WIDTH // 2, CONV_WIDTH // 2)],
                                 dimension_numbers=('NWC', 'WIO', 'NWC'),
                                 feature_group_count=CONV_CH) + dw_b
    uf = u.astype(jnp.float32)
    mu = jnp.mean(uf, axis=-1, keepdims=True)
    var = jnp.mean(jnp.square(uf - mu), axis=-1, keepdims=True)
    un = ((uf - mu) * lax.rsqrt(var + NORM_EPS) * ln_g.astype(jnp.float32) + ln_b.astype(jnp.float32)).astype(u.dtype)
    return jax.nn.silu(un) @ pw2_w + pw2_b

def setup_inputs(seed: int = 0) -> dict:
    key = jax.random.key(seed)
    ks = iter(jax.random.split(key, 48))
    f32 = jnp.float32

    def nrm(shape, scale):
        return scale * jax.random.normal(next(ks), shape, f32)

    def uni(shape, lo, hi):
        return jax.random.uniform(next(ks), shape, f32, lo, hi)

    D = D_MODEL
    return {
        'x': nrm((BATCH, SEQ, D), 1.0),
        'c': nrm((BATCH, D), 1.0),
        'ctx': nrm((BATCH, CTX_LEN, D), 1.0),
        'c_ctx': nrm((D,), 1.0),
        'ada_w': nrm((DEPTH, D, ADA_CHUNKS * D), 0.5 * D ** -0.5),
        'ada_b': nrm((DEPTH, ADA_CHUNKS * D), 0.02),
        'norm1_g': 1.0 + nrm((DEPTH, D), 0.05),
        'norm2_g': 1.0 + nrm((DEPTH, D), 0.05),
        'mlp_w1': nrm((DEPTH, D, D_FF), D ** -0.5),
        'mlp_w2': nrm((DEPTH, D_FF, D), D_FF ** -0.5),
        'mix_in_w': nrm((N_EVEN, D, IN_COLS), D ** -0.5),
        'mix_out_w': nrm((N_EVEN, D, D), D ** -0.5),
        'q_norm_g': 1.0 + nrm((N_EVEN, A_HEAD_DIM), 0.05),
        'k_norm_g': 1.0 + nrm((N_EVEN, A_HEAD_DIM), 0.05),
        'lambda_q1': nrm((N_EVEN, A_HEAD_DIM), 0.1),
        'lambda_k1': nrm((N_EVEN, A_HEAD_DIM), 0.1),
        'lambda_q2': nrm((N_EVEN, A_HEAD_DIM), 0.1),
        'lambda_k2': nrm((N_EVEN, A_HEAD_DIM), 0.1),
        'subln_g': 1.0 + nrm((N_EVEN, 2 * A_HEAD_DIM), 0.05),
        'shift_mu': uni((N_EVEN, B_COLS), 0.0, 1.0),
        'decay_w0': uni((N_EVEN, 2, B_WIDTH), -4.0, 0.0),
        'decay_up': nrm((N_EVEN, 2, DECAY_LORA, B_WIDTH), 0.5 * DECAY_LORA ** -0.5),
        'iclr_a0': nrm((N_EVEN, 2, B_WIDTH), 0.1),
        'iclr_up': nrm((N_EVEN, 2, ICLR_LORA, B_WIDTH), ICLR_LORA ** -0.5),
        'gate_up': nrm((N_EVEN, GATE_LORA, B_WIDTH), GATE_LORA ** -0.5),
        'k_k': 0.85 + nrm((N_EVEN, B_WIDTH), 0.05),
        'k_a': 1.0 + nrm((N_EVEN, B_WIDTH), 0.05),
        'r_k': nrm((N_EVEN, B_HEADS, B_HEAD_DIM), 0.1),
        'gn_w': 1.0 + nrm((N_EVEN, B_WIDTH), 0.05),
        'gn_b': nrm((N_EVEN, B_WIDTH), 0.02),
        'conv_pw1_w': nrm((N_ODD, D, 2 * CONV_CH), D ** -0.5),
        'conv_pw1_b': nrm((N_ODD, 2 * CONV_CH), 0.02),
        'conv_dw_w': nrm((N_ODD, CONV_WIDTH, CONV_CH), CONV_WIDTH ** -0.5),
        'conv_dw_b': nrm((N_ODD, CONV_CH), 0.02),
        'conv_ln_g': 1.0 + nrm((N_ODD, CONV_CH), 0.05),
        'conv_ln_b': nrm((N_ODD, CONV_CH), 0.02),
        'conv_pw2_w': nrm((N_ODD, CONV_CH, D), CONV_CH ** -0.5),
        'conv_pw2_b': nrm((N_ODD, D), 0.02),
    }

def reference(x, c, ctx, c_ctx, ada_w, ada_b, norm1_g, norm2_g, mlp_w1, mlp_w2, mix_in_w, mix_out_w,
              q_norm_g, k_norm_g, lambda_q1, lambda_k1, lambda_q2, lambda_k2, subln_g, shift_mu,
              decay_w0, decay_up, iclr_a0, iclr_up, gate_up, k_k, k_a, r_k, gn_w, gn_b,
              conv_pw1_w, conv_pw1_b, conv_dw_w, conv_dw_b, conv_ln_g, conv_ln_b, conv_pw2_w, conv_pw2_b):
    cos, sin = axial_rope_tables(x.shape[1])
    s_lat = jax.nn.silu(c)
    s_ctx = jax.nn.silu(c_ctx)
    h_lat, h_ctx = x, ctx
    for i in range(DEPTH):
        ctx_read_later = any(j % 2 == 0 for j in range(i + 1, DEPTH))
        ctx_used_here = (i % 2 == 0) or ctx_read_later
        m_lat = jnp.split((s_lat @ ada_w[i] + ada_b[i])[:, None, :], ADA_CHUNKS, axis=-1)
        hn_lat = modulate(rms_norm(h_lat, norm1_g[i]), m_lat[0], m_lat[1])
        m_ctx, hn_ctx = None, None
        if ctx_used_here:
            m_ctx = jnp.split(s_ctx @ ada_w[i] + ada_b[i], ADA_CHUNKS, axis=-1)
            hn_ctx = modulate(rms_norm(h_ctx, norm1_g[i]), m_ctx[0], m_ctx[1])
        if i % 2 == 0:
            e = i // 2
            ap = {'q_norm': q_norm_g[e], 'k_norm': k_norm_g[e], 'lq1': lambda_q1[e], 'lk1': lambda_k1[e],
                  'lq2': lambda_q2[e], 'lk2': lambda_k2[e], 'subln': subln_g[e]}
            rw = {'mu': shift_mu[e], 'w0': decay_w0[e], 'w_up': decay_up[e], 'a0': iclr_a0[e],
                  'a_up': iclr_up[e], 'g_up': gate_up[e], 'k_k': k_k[e], 'k_a': k_a[e], 'r_k': r_k[e],
                  'gn_w': gn_w[e], 'gn_b': gn_b[e]}
            lam_init = 0.8 - 0.6 * math.exp(-0.3 * i)
            y_lat, y_ctx = even_mixer(hn_lat, hn_ctx, mix_in_w[e], mix_out_w[e], ap, rw, lam_init,
                                      cos, sin, ctx_read_later)
        else:
            o = i // 2
            conv_p = (conv_pw1_w[o], conv_pw1_b[o], conv_dw_w[o], conv_dw_b[o], conv_ln_g[o], conv_ln_b[o],
                      conv_pw2_w[o], conv_pw2_b[o])
            y_lat = conformer_conv(hn_lat, *conv_p)
            y_ctx = conformer_conv(hn_ctx, *conv_p) if ctx_read_later else None
        h_lat = h_lat + m_lat[2] * y_lat
        h_lat = h_lat + m_lat[5] * squared_relu_mlp(modulate(rms_norm(h_lat, norm2_g[i]), m_lat[3], m_lat[4]),
                                                    mlp_w1[i], mlp_w2[i])
        if ctx_read_later:
            h_ctx = h_ctx + m_ctx[2] * y_ctx
            h_ctx = h_ctx + m_ctx[5] * squared_relu_mlp(modulate(rms_norm(h_ctx, norm2_g[i]), m_ctx[3], m_ctx[4]),
                                                        mlp_w1[i], mlp_w2[i])
    return h_lat


_drawn_inputs = setup_inputs


def setup_inputs(seed=0):
    import zlib

    import numpy as np

    out = dict(_drawn_inputs(seed))
    spreads = {}
    factors = {'norm1_g': 3.629,
     'q_norm_g': 8.0,
     'k_norm_g': 8.0,
     'lambda_q1': 64.0,
     'lambda_k1': 4.761,
     'lambda_q2': 4.844,
     'subln_g': 55.824,
     'decay_up': 7.17,
     'iclr_a0': 8.0,
     'k_k': 200.0,
     'k_a': 5.76,
     'gn_w': 64.0,
     'gn_b': 200.0,
     'conv_pw1_b': 64.0,
     'conv_dw_b': 53.37,
     'conv_ln_g': 163.647,
     'conv_ln_b': 200.0,
     'conv_pw2_b': 200.0,
     'norm2_g': 8.0}
    for name, (base, spread) in spreads.items():
        noise = np.random.default_rng([zlib.crc32(name.encode()), seed]).standard_normal(out[name].shape)
        drawn = base * np.exp(spread * noise) if base else spread * noise
        out[name] = jnp.asarray(drawn.astype(out[name].dtype))
    for name, factor in factors.items():
        out[name] = (out[name] * factor).astype(out[name].dtype)
    return out
```

```python
from contextlib import ExitStack

import numpy as np
import concourse.bass as bass
from concourse import mybir

ALU = mybir.AluOpType
ACT = mybir.ActivationFunctionType
F32 = mybir.dt.float32
F32R = mybir.dt.float32r
AX_X = mybir.AxisListType.X

P = 128
D = 2048
KT = D // P
SEQ = 256
TOK = 512
D_FF = 4 * D
NB = 512
CHUNK = 4
NCH = KT // CHUNK
AW = 1024
HEADS = 8
HD = 64
GRID_W = 64
IN_COLS = 6560
B0 = 3 * AW
B_COLS = IN_COLS - B0
WL0, AL0, GL0 = 3 * AW, 3 * AW + 128, 3 * AW + 256
GATE = 160
TAPS = 31
PADW = TAPS // 2
NORM_EPS = 1e-6
GN_EPS = 64e-5
C_DECAY = float(np.exp(-0.5))
LAM_INIT = 0.8 - 0.6
LEVELS = 7


def shape_constants():
    i = np.arange(P)
    c = {}
    c["ident"] = np.eye(P)
    sel = np.zeros((P, 2))
    sel[0::32, 0] = 1
    sel[1::32, 1] = 1
    c["sel"] = sel
    c["blk"] = (i[:, None] // HD == i[None, :] // HD) * 1.0
    j = np.arange(P + 1)
    mid = P // 2 - 1
    fw = (i[:, None] < j[None]) * 1.0 - (i[:, None] <= mid)
    bw = (i[:, None] >= j[None]) * 1.0 - (i[:, None] >= P - 1 - mid)
    c["tri"] = np.concatenate([fw, bw], 1)
    strict = [(i[:, None] < i[None]) * 1.0, (i[:, None] > i[None]) * 1.0]
    incl = [(i[:, None] <= i[None]) * 1.0, (i[:, None] >= i[None]) * 1.0]
    c["smask"] = np.concatenate([np.concatenate([-s, -n, s, n], 1) for s, n in zip(strict, incl)], 1)
    lev = []
    for l in range(LEVELS):
        n = 1 << l
        same = i[:, None] // (2 * n) == i[None] // (2 * n)
        low = same & (i[:, None] // n % 2 == 1) & (i[None] // n % 2 == 0)
        f = low + np.eye(P)
        b = low.T + np.eye(P)
        lev += [f.T, b.T] if l == 0 else [f, b]
    c["lmask"] = np.concatenate(lev, 1)
    rows = SEQ // GRID_W
    row = np.repeat(np.arange(rows, dtype=np.float32), GRID_W)
    col = np.tile(np.arange(GRID_W, dtype=np.float32), rows)
    nf = HD // 4
    inv = np.float32(10000.0) ** (-np.arange(nf, dtype=np.float32) / np.float32(nf))
    ang = np.stack([row[:, None] * inv, col[:, None] * inv], 1)
    ang = np.stack([ang, ang], 2).astype(np.float32)
    cos, sin = np.cos(ang), np.sin(ang)
    sin[:, :, 0] *= -1
    def lay(t):
        t = t.reshape(2, P, HD).transpose(1, 0, 2)
        t = np.repeat(t[:, :, None], 2, 2).reshape(P, 2 * 2 * HD)
        return np.concatenate([t, t], 1)
    c["cos"], c["sin"] = lay(cos), lay(sin)
    return {k: np.ascontiguousarray(v, np.float32) for k, v in c.items()}


class Steps:

    def __init__(self, eng, sem):
        self.eng, self.sem, self.base, self.n = eng, sem, 0, 0

    def inc(self, ins):
        ins.then_inc(self.sem, 1)
        self.n += 1

    def wait(self):
        self.eng.wait_ge(self.sem, self.base + self.n)

    def link(self, ins):
        self.inc(ins)
        self.wait()

    def enter(self, i, per):
        self.start, self.per = self.base + self.n, per
        self.base, self.n = i * per + self.start, 0

    def leave(self, trips):
        assert self.n == self.per, ("steps per iteration", self.n)
        self.base, self.n = self.start + trips * self.per, 0


def rows_of(v):
    return v.rearrange("(j p) -> j p", p=P)


P0 = dict(n1g0=0, n1g1=16, n2g0=32, n2g1=48, dwb=64, lng=80, lnb=96)
P0_ROWS = 112
P1 = dict(pw1b=0, mu=32, a0=60, kk=76, ka=84, rk=92, gnw=100, gnb=108)
P1_ROWS = 116
(C_MR, C_MK, C_MV, C_A0, C_A1, C_KK, C_KA, C_RK, C_GW, C_GB) = range(10)
C_HR, C_OR, C_OKA = 10, 13, 16
C_N = 17

PE_F = 3
MIX_M = 13
ADA_A, ADA_T, ADA_R = 8, 1, 4
Q_AT = ADA_A
Q_RW = Q_AT + ADA_T * HEADS
Q_ALL = Q_RW + ADA_R * HEADS
SCAN = [[0, 1, 2, 3], [1, 0, 3, 2]]
RW_DVE = 35


def rwkv_memory(nc):
    t = {}
    with ExitStack() as s:
        def sb(name, *shape, dt=F32):
            t[name] = s.enter_context(nc.sbuf_tensor("rw_" + name, list(shape), dt))
        sb("smask", P, 2, 4 * P)
        sb("lmask", P, LEVELS, 2, P)
        sb("tri", P, 2, P + 1)
        sb("blk", P, P)
        sb("table", P, HEADS, C_N)
        sb("cur", P, C_N)
        sb("rkv", P, 3, 2, SEQ + 2)
        sb("wup", P, P)
        sb("aup", P, P)
        sb("gup", P, 2, P)
        sb("w0", 1, 2, P)
        sb("al", P, TOK)
        sb("th", P, TOK)
        sb("sg", P, 2, SEQ)
        sb("r", P, SEQ)
        sb("k", P, TOK)
        sb("v", P, TOK)
        sb("kk", P, TOK)
        sb("t12", P, 2, TOK)
        sb("a", P, 2, TOK)
        sb("kd", P, 2, TOK)
        sb("lw", P, 2, 4, P)
        sb("ep", P, 2, 4, P + 1)
        sb("en", P, 2, 4, P + 1)
        sb("pm", P, 2, 4, 2)
        sb("kx", P, 2, 4, 2, P)
        sb("kh", P, 2, 4, P)
        sb("bh", P, 2, 4, P)
        sb("vt", P, 4, P)
        sb("kht", P, 2, 4, P)
        sb("bht", P, 2, 4, P)
        sb("scc", P, 2, 4, 2 * P)
        sb("scl", P, 2, 4, 4 * P)
        sb("nt", P, 2, 4, P)
        sb("tb", P, 2, 4, P)
        sb("tt", P, 4, 4, P)
        sb("rh", P, 4, HD)
        sb("u", P, 4, HD)
        sb("sp", P, 2, HD)
        sb("o", P, SEQ)
    return t


def attention_memory(nc):
    t = {}
    with ExitStack() as s:
        def sb(name, *shape, dt=F32):
            t[name] = s.enter_context(nc.sbuf_tensor("at_" + name, list(shape), dt))
        sb("cos", P, 4, P)
        sb("sin", P, 4, P)
        sb("gain", P, 6, P)
        sb("lq", P, 4, HD)
        sb("sub", P, 1)
        sb("qk", P, 6, P)
        sb("v", P, 4, P)
        sb("t1", P, 6, P)
        sb("t2", P, 6, P)
        sb("qkr", P, 6, P)
        sb("kT", P, TOK)
        sb("qT", P, SEQ)
        sb("e", P, 4, TOK)
        sb("p", P, 2, TOK)
        sb("pT", P, 4, SEQ)
        sb("on", P, 2, P)
        sb("junk", P, 2, P)
        sb("st", P, 64)
        sb("lam", P, 8)
    return t


def build_trunk(nc, a, out):
    with ExitStack() as top:
        def sb(stack, name, shape, dt=F32):
            return stack.enter_context(nc.sbuf_tensor(name, shape, dt))

        def sem(name):
            return top.enter_context(nc.semaphore(name))

        qkv_d = nc.dram_tensor("qkv_scratch", [TOK, 3 * AW], F32).ap()
        rwkv_d = nc.dram_tensor("rwkv_scratch", [B_COLS, TOK], F32).ap()
        mod_d = nc.dram_tensor("mod_scratch", [2, 2, 6 * D], F32).ap()

        ps = top.enter_context(nc.psum_tensor("ps", [P, 8, NB], F32))
        ADA_ACC, ADA_SUM = 4, 5
        raw = sb(top, "raw", [P, NCH, CHUNK, NB])
        hbuf = sb(top, "hbuf", [P, 2, D])
        yT = hbuf[:, :, :].rearrange("p a (k t) -> p (a k) t", t=SEQ)
        gate = sb(top, "gate", [P, D])
        tmpa = sb(top, "tmpa", [P, 2, NB])
        part = sb(top, "part", [P, NB])
        line = sb(top, "line", [P, 4, NB])
        asum = line[32:34, 3, :]
        s32 = sb(top, "s32", [P, KT, 32])
        ident = sb(top, "ident_t", [P, P])
        ones = sb(top, "ones_t", [P, P])
        sel = sb(top, "sel_t", [P, 2])
        mrow = sb(top, "mrow", [P, P])
        pcol = sb(top, "pcol", [P, 2, P])
        mcol = sb(top, "mcol", [P, 96])
        gcol = sb(top, "gcol", [P, 5, 16])
        dwc = sb(top, "dwc", [P, KT, TAPS])
        small = sb(top, "small", [P, 32])
        cvec = sb(top, "cvec", [P, 4, KT])
        epsc = sb(top, "epsc", [P, 2])
        prow = [hbuf[:, 0, 0:P], hbuf[:, 0, P:2 * P]]
        dwr = gate[0:TAPS, :]
        with ExitStack() as s:
            x4 = sb(s, "x4", [P, 4, D])
            xn4 = sb(s, "xn4", [P, 4, D])
        with ExitStack() as s:
            split_hi = sb(s, "split_hi", [P, NCH, CHUNK, NB], F32R)
            split_lo = sb(s, "split_lo", [P, NCH, CHUNK, NB], F32R)
            with ExitStack() as t:
                mx_hi = sb(t, "mx_hi", [P, KT, TOK], F32R)
                mx_lo = sb(t, "mx_lo", [P, KT, TOK], F32R)
            with ExitStack() as t:
                diag = sb(t, "diag", [P, 8, PE_F, P])
            xa_hi = sb(s, "xa_hi", [P, KT, SEQ], F32R)
            xa_lo = sb(s, "xa_lo", [P, KT, SEQ], F32R)
            with ExitStack() as t:
                hT_hi = sb(t, "hT_hi", [P, KT, SEQ], F32R)
                hT_lo = sb(t, "hT_lo", [P, KT, SEQ], F32R)
            with ExitStack() as t:
                xn2 = sb(t, "xn2", [P, 2, D])
            with ExitStack() as t:
                gpad = sb(t, "gpad", [P, KT, SEQ + 2 * PADW])
                cu = sb(t, "cu", [P, KT, SEQ])
        rw = rwkv_memory(nc)
        at = attention_memory(nc)
        stage = hbuf[:, 0, :].rearrange("p (b n) -> p b n", n=NB)

        raw_in = [sem(f"raw_in{c}") for c in range(NCH)]
        hi_done, lo_done = sem("hi_done"), sem("lo_done")
        pe_chunk = sem("pe_chunk")
        pe_ada = sem("pe_ada")
        ab_in = [sem(f"ab_in{i}") for i in range(ADA_R)]
        ada_part, ada_sum, ada_out, ada_st = sem("ada_part"), sem("ada_sum"), sem("ada_out"), sem("ada_st")
        cst_in, cv_in, prow_in, x_in, mrow_in = sem("cst_in"), sem("cv_in"), sem("prow_in"), sem("x_in"), sem("mrow_in")
        init_done, sig_done, s_ready = sem("init_done"), sem("sig_done"), sem("s_ready")
        pt_ps, pt_ok = sem("pt_ps"), sem("pt_ok")
        mt_ps, mcol_ok = sem("mt_ps"), sem("mcol_ok")
        norm_std, norm_xn, tr_ps, tr_ts, tr_hi, tr_lo = (sem(n) for n in ("norm_std", "norm_xn", "tr_ps", "tr_ts", "tr_hi", "tr_lo"))
        norm_sq = sem("norm_sq")
        mix_ev_a, mix_ev_d = sem("mix_ev_a"), sem("mix_ev_d")
        mix_st = [sem(f"mix_st{b}") for b in range(4)]
        dve_s, act_s = sem("dve_steps"), sem("act_steps")
        bar = sem("stage_end")
        out_done = sem("out_done")
        pool_go = sem("pool_go")

        w = {"in": a["mix_in_w"][0], "out": a["mix_out_w"][0], "pw1": a["conv_pw1_w"][0], "pw2": a["conv_pw2_w"][0]}

        def ada_src(layer, col):
            return a["ada_w"][layer].rearrange("(p k) n -> p k n", k=KT)[:, :, bass.ds(col, NB)]

        def weight_src(mat, col, n=NB, row=0):
            return mat[bass.ds(row, D), bass.ds(col, n)].rearrange("(k p) n -> p k n", p=P)

        def send(sp, src, n, before):
            for c in range(NCH):
                if before is not None:
                    kind, i = before
                    if kind == "product":
                        sp.wait_ge(hi_done, i * 4 + (c + 1))
                        sp.wait_ge(lo_done, i * 4 + (c + 1))
                    else:
                        sp.wait_ge(pe_ada, i * 4 + (c + 1))
                sp.dma_start(raw[:, c, :, 0:n], src[:, c * CHUNK:(c + 1) * CHUNK, :]).then_inc(raw_in[c], 16)

        def rwkv_ada(i, j):
            return (0, i * NB + Q_RW * NB) if j == 0 else (1, i * ((ADA_R - 1) * NB) + (j - 1) * NB)

        def send_ada(sp, layer, col, q, slot, before):
            send(sp, ada_src(layer, col), NB, before)
            if not (isinstance(q, int) and q < 2):
                sp.wait_ge(ada_sum, q)
            sp.dma_start(line[0:1, slot, :], a["ada_b"][layer:layer + 1, bass.ds(col, NB)]).then_inc(ab_in[slot], 16)

        def pe_ada_chunk(pe, q, b, c):
            if c == 0 and not (isinstance(q, int) and q == 0):
                pe.wait_ge(ada_part, q)
            pe.wait_ge(raw_in[c], b * 16 + 16)
            for kk in range(CHUNK):
                mm = pe.matmul(ps[32 * kk:32 * kk + 32, ADA_ACC, :], s32[:, c * CHUNK + kk, :], raw[:, c, kk, :],
                               start=(c == 0), stop=(c == NCH - 1))
            mm.then_inc(pe_ada, 1)

        def pe_ada_sum(pe, q, slot, loads):
            pe.wait_ge(ada_part, q + 1)
            pe.wait_ge(ab_in[slot], loads * 16)
            if not (isinstance(q, int) and q == 0):
                pe.wait_ge(ada_out, q)
            pe.matmul(ps[32:34, ADA_SUM, :], sel[:, :], part[:, :], start=True, stop=False)
            pe.matmul(ps[32:34, ADA_SUM, :], ones[0:1, 0:2], line[0:1, slot, :], start=False, stop=True).then_inc(ada_sum, 1)

        def act_ada(act, layer, col, q):
            act_ada_part(act, q)
            act_ada_store(act, layer, col, q)

        def act_ada_part(act, q):
            act.wait_ge(pe_ada, q * 4 + 4)
            if not (isinstance(q, int) and q == 0):
                act.wait_ge(ada_sum, q)
            nc.scalar.activation(part[:, :], ps[:, ADA_ACC, :], ACT.Copy).then_inc(ada_part, 1)

        def act_ada_store(act, layer, col, q):
            act.wait_ge(ada_sum, q + 1)
            if not (isinstance(q, int) and q == 0):
                act.wait_ge(ada_st, q * 16)
            nc.scalar.activation(asum, ps[32:34, ADA_SUM, :], ACT.Copy).then_inc(ada_out, 1)
            act.wait_ge(ada_out, q + 1)
            act.dma_start(mod_d[layer, :, bass.ds(col, NB)], asum).then_inc(ada_st, 16)

        def act_split(act, m, b, n=NB):
            for c in range(NCH):
                act.wait_ge(raw_in[c], b * 16 + 16)
                if not (isinstance(m, int) and m == 0):
                    act.wait_ge(pe_chunk, m * 4 + (c - 3))
                nc.scalar.activation(split_hi[:, c, :, 0:n], raw[:, c, :, 0:n], ACT.Copy).then_inc(hi_done, 1)

        def dve_split(dve, m, b, n=NB):
            for c in range(NCH):
                dve.wait_ge(hi_done, m * 4 + (c + 1))
                nc.vector.tensor_tensor(split_lo[:, c, :, 0:n], raw[:, c, :, 0:n], split_hi[:, c, :, 0:n],
                                        ALU.subtract).then_inc(lo_done, 1)

        def pe_product(pe, m, groups, before_chunk=None, bank_free=None):
            for c in range(NCH):
                if before_chunk:
                    before_chunk(c)
                pe.wait_ge(hi_done, m * 4 + (c + 1))
                pe.wait_ge(lo_done, m * 4 + (c + 1))
                for g, (stationary, wc, x_hi, x_lo, dst, opens) in enumerate(groups):
                    if c == 0 and bank_free:
                        bank_free(g)
                    for kk in range(CHUNK):
                        k = c * CHUNK + kk
                        first, last = k == 0, k == KT - 1
                        wh, wl = split_hi[:, c, kk, wc[0]:wc[1]], split_lo[:, c, kk, wc[0]:wc[1]]
                        if stationary:
                            seq = [(wh, x_hi(k)), (wh, x_lo(k)), (wl, x_hi(k))]
                        else:
                            seq = [(x_hi(k), wh), (x_hi(k), wl), (x_lo(k), wh)]
                        for i, (l, r) in enumerate(seq):
                            mm = pe.matmul(dst, l, r, start=(first and i == 0 and opens), stop=(last and i == 2),
                                           skip_group_check=True)
                mm.then_inc(pe_chunk, 1)

        def pe_transposes(pe, n0, src, tiles):
            per = NB // (tiles * P)
            for i in range(KT // per):
                n = n0 + i
                if n >= 4:
                    pe.wait_ge(tr_ts, n - 3)
                for j in range(per):
                    for t in range(tiles):
                        k = i * per + j
                        o = (j * tiles + t) * P
                        tr = pe.transpose(ps[:, n % 4, o:o + P], src[:, t, k * P:(k + 1) * P], ident[:, :])
                tr.then_inc(tr_ps, 1)

        def dve_modulate(dve, n0, tiles, cols, hi, lo):
            per = NB // (tiles * P)
            nb = KT // per

            def low(i):
                n = n0 + i
                dve.wait_ge(tr_hi, n + 1)
                nc.vector.tensor_tensor(lo(i), tmpa[:, n % 2, :].rearrange("p (a t) -> p a t", a=per), hi(i),
                                        ALU.subtract).then_inc(tr_lo, 1)

            for i in range(nb):
                n = n0 + i
                dve.wait_ge(tr_ps, n + 1)
                if n >= 2:
                    dve.wait_ge(tr_lo, n - 1)
                for seg in range(2):
                    k, (g, sh) = (i, cols[seg]) if per == 1 else (2 * i + seg, cols[0])
                    ins = nc.vector.tensor_scalar(tmpa[:, n % 2, seg * 256:seg * 256 + 256],
                                                  ps[:, n % 4, seg * 256:seg * 256 + 256],
                                                  g[:, k:k + 1], sh[:, k:k + 1], ALU.mult, ALU.add)
                ins.then_inc(tr_ts, 1)
                if i:
                    low(i - 1)
            low(nb - 1)

        def act_high(act, n0, tiles, hi):
            per = NB // (tiles * P)
            for i in range(KT // per):
                n = n0 + i
                act.wait_ge(tr_ts, n + 1)
                nc.scalar.activation(hi(i), tmpa[:, n % 2, :].rearrange("p (a t) -> p a t", a=per), ACT.Copy).then_inc(tr_hi, 1)

        def act_stats(act, q, x, xn, tiles):
            for t in range(tiles):
                ins = nc.scalar.activation(xn[:, t, :], x[:, t, :], ACT.Square, accum_out=small[:, t:t + 1])
            ins.then_inc(norm_sq, 1)
            act.wait_ge(norm_sq, q + 1)
            nc.scalar.activation(small[:, 4:4 + tiles], small[:, 0:tiles], ACT.Sqrt, scale=1.0 / D,
                                 bias=epsc[:, 0:1]).then_inc(norm_std, 1)

        def dve_scale(dve, q, steps, x, xn, tiles):
            dve.wait_ge(norm_std, q + 1)
            steps.link(nc.vector.reciprocal(small[:, 8:8 + tiles], small[:, 4:4 + tiles]))
            for t in range(tiles):
                ins = nc.vector.tensor_scalar(xn[:, t, :], x[:, t, :], small[:, 8 + t:9 + t], None, ALU.mult)
            ins.then_inc(norm_xn, 1)

        def stage_end(eng, n):
            eng.drain().then_inc(bar, 1)
            eng.wait_ge(bar, 4 * n)

        def mix_bank(m, lane):
            return lane + 4 * ((m + 1) % 2)

        def mix_out(m):
            if m < 6:
                tts = [2, 3] if m < 2 else [0, 1, 2, 3]
                banks = [0, 2] if m < 2 else [0, 1, 2, 3]
                return [(b, qkv_d[t * P:(t + 1) * P, m * NB:(m + 1) * NB], P, 0) for b, t in zip(banks, tts)]
            res = []
            for j in range(4):
                r0 = (m - 6) * NB + j * P
                rows = min(P, B_COLS - r0)
                t0 = SEQ if m < 8 or r0 >= GL0 else 0
                res.append((j, rwkv_d[r0:r0 + rows, t0:TOK], rows, t0))
            return res

        def mix_groups(m):
            g = []
            for b, dst, rows, t0 in mix_out(m):
                if m < 6:
                    t = (2 + b // 2) if m < 2 else b
                    g.append((False, (0, NB), lambda k, t=t: mx_hi[:, k, t * P:(t + 1) * P],
                              lambda k, t=t: mx_lo[:, k, t * P:(t + 1) * P], ps[:, mix_bank(m, b), :], True))
                else:
                    g.append((True, (b * P, (b + 1) * P), lambda k, t0=t0: mx_hi[:, k, t0:TOK],
                              lambda k, t0=t0: mx_lo[:, k, t0:TOK], ps[:, mix_bank(m, b), 0:TOK - t0], True))
            return g

        def evacuated(m, bank):
            mine = 0 if bank < 2 else 2
            return sum(1 for n in range(m + 1) for b, *_ in mix_out(n) if mine <= b < mine + 2 and (n < m or b <= bank))

        def stored(m, bank):
            return sum(1 for n in range(m + 1) for b, *_ in mix_out(n) if b == bank)


        at_cst, at_init, at_lam = sem("at_cst"), sem("at_init"), sem("at_lam")
        at_qk_in, at_v_in = sem("at_qk_in"), sem("at_v_in")
        at_ss, at_std, at_qkr, at_tp, at_kT, at_qT = (sem(n) for n in ("at_ss", "at_std", "at_qkr", "at_tp", "at_kT", "at_qT"))
        at_sc, at_mx, at_e, at_p, at_pt, at_pT_a, at_pT_d = (sem(n) for n in ("at_sc", "at_mx", "at_e", "at_p", "at_pt", "at_pT_a", "at_pT_d"))
        at_o, at_std2, at_on, at_ot, at_y = (sem(n) for n in ("at_o", "at_std2", "at_on", "at_ot", "at_y"))
        SC_BANKS = [2, 3, 6, 7]

        def col_of(name, i=0, n=1):
            if name in P0:
                return pcol[:, 0, P0[name] + i:P0[name] + i + n]
            return pcol[:, 1, P1[name] + i:P1[name] + i + n]


        rws = {n: sem("rw_" + n) for n in (
            "cst", "cst2", "lora", "init", "in", "gin", "k", "sq", "nrm_ps", "nrm", "a_ps", "a", "z_ps", "lw",
            "cum_ps", "cum", "v", "prod", "tr_ps", "tr", "sc_ps", "sc", "nt", "x_ps", "x", "t_ps", "t", "tt_ps", "tt",
            "rh_ps", "rh", "u_ps", "u", "o_ps", "o", "st_ps", "sp", "mean_ps", "om", "sqo", "var_ps", "std", "pr",
            "bon_ps", "g_ps", "y")}
        GB = [[0, 1, 2], [3, 6, 7]]
        SCB = [2, 3, 6, 7, 0, 1]
        RHB = [0, 1]
        LAT = [False, False, True, True]

        def bc(x, n):
            return x.rearrange("p d (o t) -> p d o t", o=1).to_broadcast([P, x.shape[1], n, x.shape[2]])

        def scores_of(c):
            return rw["scl"][:, c - 2, :, :] if LAT[c] else rw["scc"][:, c, :, :]

        def bt(c, inst):
            return scores_of(c)[:, inst, 2 * P:3 * P] if LAT[c] else scores_of(c)[:, inst, P:2 * P]

        flat = lambda n: rw[n][:, :, :, :].rearrange("p d c s -> p (d c s)")
        lora_in = flat("ep").rearrange("p (j s t) -> p j s t", j=2, s=2)
        gate_rows = flat("en")[:, 0:2 * (SEQ + 2)].rearrange("p (s t) -> p s t", s=2)

        def rwkv_pool(pool):
            stage_end(pool, 2)
            R = rw["rkv"]
            with pool.Fori(0, HEADS) as i:
                pool.wait_ge(rws["v"], i + 1)
                pool.wait_ge(rws["z_ps"], i * 2 + 2)
                pool.wait_ge(rws["a_ps"], i * 2 + 2)
                pool.sem_inc(pool_go, 1)
                for j, r0 in ((1, AW), (2, 2 * AW)):
                    pool.dma_start(R[:, j, :, 1:SEQ + 1], rwkv_d[bass.ds(i * P + r0, P), :].rearrange("p (s t) -> p s t", s=2)).then_inc(rws["in"], 16)
                pool.dma_start(R[:, 0, 1, 1:SEQ + 1], rwkv_d[bass.ds(i * P, P), SEQ:TOK]).then_inc(rws["in"], 16)
                pool.dma_start(rw["wup"][:, :], a["decay_up"][0].rearrange("d r n -> (d r) n")[:, bass.ds(i * P, P)]).then_inc(rws["in"], 16)
                pool.dma_start(rw["aup"][:, :], a["iclr_up"][0].rearrange("d r n -> (d r) n")[:, bass.ds(i * P, P)]).then_inc(rws["in"], 16)
                pool.dma_start(rw["w0"][:, :, :], a["decay_w0"][:, :, bass.ds(i * P, P)]).then_inc(rws["in"], 16)
                pool.wait_ge(rws["g_ps"], i + 1)
                pool.sem_inc(pool_go, 1)
                pool.dma_start(rw["gup"][:, 0, :], a["gate_up"][0, 0:P, bass.ds(i * P, P)]).then_inc(rws["gin"], 16)
                pool.dma_start(rw["gup"][0:32, 1, :], a["gate_up"][0, P:GATE, bass.ds(i * P, P)]).then_inc(rws["gin"], 16)

        def rwkv_act(act, steps):
            stage_end(act, 2)
            W = rws
            for j, r0 in enumerate((WL0, AL0)):
                act.dma_start(lora_in[:, j, :, 1:SEQ + 1], rwkv_d[r0:r0 + P, :].rearrange("p (s t) -> p s t", s=2)).then_inc(rws["lora"], 16)
            act.dma_start(gate_rows[:, 0, 1:SEQ + 1], rwkv_d[GL0:GL0 + P, SEQ:TOK]).then_inc(rws["lora"], 16)
            act.dma_start(gate_rows[0:32, 1, 1:SEQ + 1], rwkv_d[GL0 + P:GL0 + GATE, SEQ:TOK]).then_inc(rws["lora"], 16)
            for n in ("tri", "blk", "smask", "lmask"):
                t = rw[n]
                dst = t[:, :] if n == "blk" else (t[:, :, :, :] if n == "lmask" else t[:, :, :])
                src = a[n]
                if n == "smask" or n == "tri":
                    src = src.rearrange("p (d n) -> p d n", d=2)
                if n == "lmask":
                    src = src.rearrange("p (l d n) -> p l d n", l=LEVELS, d=2)
                act.dma_start(dst, src).then_inc(rws["cst"], 16)
            act.wait_ge(W["init"], 1)
            nc.scalar.activation(rw["th"][:, :], rw["t12"][:, 0, :], ACT.Tanh).then_inc(W["cst2"], 1)
            act.wait_ge(W["init"], 2)
            nc.scalar.activation(rw["sg"][:, 0, :], rw["t12"][:, 1, 0:SEQ], ACT.Sigmoid).then_inc(W["cst2"], 1)
            nc.scalar.activation(rw["sg"][0:32, 1, :], rw["t12"][0:32, 1, SEQ:TOK], ACT.Sigmoid).then_inc(W["cst2"], 1)
            with act.Fori(0, HEADS) as i:
                act.wait_ge(W["k"], i + 1)
                nc.scalar.activation(rw["t12"][:, 0, :], rw["k"][:, :], ACT.Square, scale=rw["cur"][:, C_KK:C_KK + 1]).then_inc(W["sq"], 1)
                for d in range(2):
                    act.wait_ge(W["a_ps"], i * 2 + (d + 3))
                    nc.scalar.activation(rw["a"][:, d, :], ps[:, 1 + d, :], ACT.Sigmoid,
                                         bias=rw["cur"][:, C_A0 + d:C_A0 + d + 1]).then_inc(W["a"], 1)
                for d in range(2):
                    act.wait_ge(W["z_ps"], i * 2 + (d + 3))
                    nc.scalar.activation(rw["lw"][:, d, :, :], ps[:, (3, 6)[d], :].rearrange("p (t s) -> p t s", t=4),
                                         ACT.Sigmoid).then_inc(W["lw"], 1)
                act.wait_ge(W["nrm_ps"], i + 1)
                nc.scalar.activation(rw["t12"][:, 1, :], ps[:, 0, :], ACT.Sqrt).then_inc(W["nrm"], 1)
                for n in range(4):
                    d, pr = n // 2, n % 2
                    act.wait_ge(W["cum_ps"], i * 4 + (n + 1))
                    src = ps[:, (0, 7, 1, 2)[n], 0:2 * (P + 1)].rearrange("p (t s) -> p t s", t=2)
                    nc.scalar.activation(rw["ep"][:, d, 2 * pr:2 * pr + 2, :], src, ACT.Exp, scale=-C_DECAY)
                    nc.scalar.activation(rw["en"][:, d, 2 * pr:2 * pr + 2, :], src, ACT.Exp, scale=C_DECAY).then_inc(W["cum"], 1)
                for n, (b, dst) in enumerate([(3, rw["vt"][:, :, :]), (6, rw["kht"][:, 0, :, :]), (7, rw["kht"][:, 1, :, :]),
                                              (0, rw["bht"][:, 0, :, :]), (1, rw["bht"][:, 1, :, :])]):
                    act.wait_ge(W["tr_ps"], i * 5 + (n + 1))
                    nc.scalar.activation(dst, ps[:, b, :].rearrange("p (t s) -> p t s", t=4), ACT.Copy,
                                         scale=-1.0 if n >= 3 else 1.0).then_inc(W["tr"], 1)
                    if n == 0:
                        act_ada_part(act, i * ADA_R + Q_RW)
                act_ada_store(act, *rwkv_ada(i, 0), i * ADA_R + Q_RW)
                four = lambda b: ps[:, b, :].rearrange("p (t s) -> p t s", t=4)
                for p in range(2):
                    for lev in range(LEVELS):
                        if lev < LEVELS - 1:
                            for g in range(2):
                                act.wait_ge(W["t_ps"], i * 24 + (p * 12 + lev * 2 + g + 1))
                                nc.scalar.activation(rw["tb"][:, g, :, :], four(GB[g][1]), ACT.Copy).then_inc(W["t"], 1)
                        if lev:
                            for g in range(2):
                                act.wait_ge(W["tt_ps"], i * 24 + (p * 12 + (lev - 1) * 2 + g + 1))
                                nc.scalar.activation(rw["tt"][:, 2 * p + g, :, :], four(GB[g][2]), ACT.Copy).then_inc(W["tt"], 1)
                for c in range(4):
                    act.wait_ge(W["rh_ps"], i * 4 + (c + 1))
                    nc.scalar.activation(rw["rh"][:, :, :].rearrange("p (d h) s -> p h d s", d=2),
                                         ps[:, 0:2, 0:2 * HD].rearrange("p h (d s) -> p h d s", d=2),
                                         ACT.Copy).then_inc(W["rh"], 1)
                    if c:
                        act_ada(act, *rwkv_ada(i, c), i * ADA_R + (Q_RW + c))
                act.wait_ge(W["om"], i + 1)
                nc.scalar.activation(rw["t12"][:, 0, 0:SEQ], rw["o"][:, :], ACT.Square).then_inc(W["sqo"], 1)
                act.wait_ge(W["var_ps"], i + 1)
                nc.scalar.activation(rw["t12"][:, 0, SEQ:TOK], ps[:, 7, 0:SEQ], ACT.Sqrt, scale=1.0 / HD, bias=epsc[:, 1:2]).then_inc(W["std"], 1)

        def rwkv_dve(dve, steps):
            W = rws
            stage_end(dve, 2)
            V = nc.vector
            R, T, cur = rw["rkv"], rw["table"], rw["cur"]
            steps.inc(V.memset(R[:, :, :, 0:1], 0.0))
            steps.inc(V.memset(R[:, :, :, SEQ + 1:SEQ + 2], 0.0))
            for rows in (lora_in, gate_rows.rearrange("p (o s) t -> p o s t", o=1)):
                steps.inc(V.memset(rows[:, :, :, 0:1], 0.0))
                steps.inc(V.memset(rows[:, :, :, SEQ + 1:SEQ + 2], 0.0))
            steps.wait()
            dve.sem_inc(W["v"], 1)
            dve.sem_inc(W["z_ps"], 2)
            dve.sem_inc(W["a_ps"], 2)
            dve.sem_inc(W["g_ps"], 1)
            dve.sem_inc(W["y"], 1)
            for c, (name, o) in enumerate([("mu", 0), ("mu", 8), ("mu", 16), ("a0", 0), ("a0", 8), ("kk", 0), ("ka", 0),
                                           ("rk", 0), ("gnw", 0), ("gnb", 0)]):
                steps.inc(V.tensor_copy(T[:, :, c], col_of(name, o, 8)))
            steps.wait()
            steps.inc(V.tensor_scalar(T[:, :, C_HR:C_HR + 3], T[:, :, 0:3], 0.5, None, ALU.mult))
            steps.inc(V.tensor_scalar(T[:, :, C_OR:C_OR + 3], T[:, :, 0:3], -1.0, 1.0, ALU.mult, ALU.add))
            steps.inc(V.tensor_scalar(T[:, :, C_OKA:C_OKA + 1], T[:, :, C_KA:C_KA + 1], -1.0, 1.0, ALU.mult, ALU.add))
            steps.inc(V.tensor_scalar(cur[:, 0:4], col_of("mu", 24, 4), 0.5, None, ALU.mult))
            steps.inc(V.tensor_scalar(cur[:, 4:8], col_of("mu", 24, 4), -1.0, 1.0, ALU.mult, ALU.add))
            steps.wait()

            def shift(dst, src, tmp, half_mu, one_mu):
                steps.link(V.tensor_tensor(tmp, src[..., 0:SEQ], src[..., 2:SEQ + 2], ALU.add))
                steps.link(V.tensor_scalar(tmp, tmp, half_mu, None, ALU.mult))
                return V.scalar_tensor_tensor(out=dst, in0=src[..., 1:SEQ + 1], scalar=one_mu, in1=tmp, op0=ALU.mult, op1=ALU.add)

            two = lambda x: x.rearrange("p (s t) -> p s t", s=2)
            kd0 = rw["kd"][:, 0, :]
            dve.wait_ge(W["lora"], 64)
            shift(two(rw["t12"][:, 0, :]), lora_in[:, 0, :, :], two(kd0), cur[:, 0:1], cur[:, 4:5]).then_inc(W["init"], 1)
            dve.wait_ge(W["init"], 1)
            steps.inc(shift(two(rw["al"][:, :]), lora_in[:, 1, :, :], two(kd0), cur[:, 1:2], cur[:, 5:6]))
            steps.wait()
            steps.inc(shift(rw["t12"][:, 1, 0:SEQ], gate_rows[:, 0, :], kd0[:, 0:SEQ], cur[:, 2:3], cur[:, 6:7]))
            steps.wait()
            shift(rw["t12"][0:32, 1, SEQ:TOK], gate_rows[0:32, 1, :], kd0[0:32, 0:SEQ], cur[0:32, 3:4], cur[0:32, 7:8]).then_inc(W["init"], 1)
            dve.wait_ge(W["init"], 2)
            dve.wait_ge(W["cst2"], 3)
            dve.wait_ge(W["cst"], 64)
            t12 = rw["t12"]
            four = lambda x: x.rearrange("p (t s) -> p t s", t=4)
            EX, IN = [0, 1], [1, 0]
            ST, EN = [0, P], [P, 0]
            with dve.Fori(0, HEADS) as i:
                steps.enter(i, RW_DVE)
                steps.link(V.tensor_copy(cur[:, :], T[:, bass.ds(i, 1), :].rearrange("p a c -> p (a c)")))
                dve.wait_ge(W["in"], i * 96 + 96)
                shift(two(rw["k"][:, :]), R[:, 1, :, :], two(kd0), cur[:, C_HR + 1:C_HR + 2], cur[:, C_OR + 1:C_OR + 2]).then_inc(W["k"], 1)
                kd1 = rw["kd"][:, 1, :]
                steps.inc(shift(rw["r"][:, :], R[:, 0, 1, :], kd1[:, 0:SEQ], cur[:, C_HR:C_HR + 1], cur[:, C_OR:C_OR + 1]))
                steps.wait()
                shift(two(rw["v"][:, :]), R[:, 2, :, :], two(kd1), cur[:, C_HR + 2:C_HR + 3], cur[:, C_OR + 2:C_OR + 3]).then_inc(W["v"], 1)
                dve.wait_ge(W["k"], i + 1)
                dve.wait_ge(W["v"], i + 2)
                dve.wait_ge(W["a"], i * 2 + 2)
                steps.link(V.tensor_scalar(rw["kd"][:, :, :], rw["a"][:, :, :], cur[:, C_KA:C_KA + 1], cur[:, C_OKA:C_OKA + 1], ALU.mult, ALU.add))
                kb = rw["k"][:, :].rearrange("p (o t) -> p o t", o=1).to_broadcast([P, 2, TOK])
                steps.inc(V.tensor_tensor(rw["kd"][:, :, :], rw["kd"][:, :, :], kb, ALU.mult))
                dve.wait_ge(W["nrm"], i + 1)
                steps.link(V.tensor_scalar(t12[:, 1, :], t12[:, 1, :], 1e-12, None, ALU.max))
                steps.link(V.reciprocal(t12[:, 0, :], t12[:, 1, :]))
                steps.link(V.scalar_tensor_tensor(out=rw["kk"][:, :], in0=rw["k"][:, :], scalar=cur[:, C_KK:C_KK + 1],
                                                  in1=t12[:, 0, :], op0=ALU.mult, op1=ALU.mult))
                kkb = rw["kk"][:, :].rearrange("p (o t) -> p o t", o=1).to_broadcast([P, 2, TOK])
                steps.link(V.tensor_tensor(rw["a"][:, :, :], rw["a"][:, :, :], kkb, ALU.mult))
                dve.wait_ge(W["cum"], i * 4 + 4)
                for d in range(2):
                    ep, en = rw["ep"][:, d, :, :], rw["en"][:, d, :, :]
                    steps.inc(V.tensor_tensor(rw["kh"][:, d, :, :], four(rw["kd"][:, d, :]), en[:, :, IN[d]:IN[d] + P], ALU.mult))
                    steps.inc(V.tensor_tensor(rw["bh"][:, d, :, :], four(rw["a"][:, d, :]), en[:, :, IN[d]:IN[d] + P], ALU.mult))
                    steps.inc(V.tensor_tensor(rw["kx"][:, d, :, 0, :], four(rw["kk"][:, :]), ep[:, :, EX[d]:EX[d] + P], ALU.mult))
                    steps.inc(V.tensor_tensor(rw["kx"][:, d, 2:4, 1, :], two(rw["r"][:, :]),
                                              ep[:, 2:4, IN[d]:IN[d] + P], ALU.mult))
                steps.wait()
                for c in range(3):
                    for d in range(2):
                        ins = V.tensor_tensor(rw["pm"][:, d, c, 0:1], rw["ep"][:, d, SCAN[d][c], EN[d]:EN[d] + 1],
                                              rw["en"][:, d, SCAN[d][c + 1], ST[d]:ST[d] + 1], ALU.mult)
                ins.then_inc(W["prod"], 1)
                n = 0
                for c in range(4):
                    for inst in range(4):
                        d = inst // 2
                        dve.wait_ge(W["sc_ps"], i * 16 + (n + 1))
                        m = rw["smask"][:, d, :].rearrange("p (q t) -> p q t", q=4)
                        if LAT[c]:
                            ins = V.tensor_tensor(rw["scl"][:, c - 2, inst, :].rearrange("p (q t) -> p q t", q=4),
                                                  ps[:, SCB[n % 6], :].rearrange("p (q t) -> p q t", q=4), m, ALU.mult)
                        else:
                            ins = V.tensor_tensor(rw["scc"][:, c, inst, :].rearrange("p (q t) -> p q t", q=2),
                                                  ps[:, SCB[n % 6], 0:2 * P].rearrange("p (q t) -> p q t", q=2), m[:, 0:4:2, :], ALU.mult)
                        ins.then_inc(W["sc"], 1)
                        n += 1
                xb = t12[:, :, :].rearrange("p g (t s) -> p g t s", t=4)
                dh = lambda x: x.rearrange("p (d h) s -> p d h s", d=2)
                for p in range(2):
                    dve.wait_ge(W["sc"], i * 16 + (8 * p + 8))
                    for g in range(2):
                        c = 2 * p + g
                        steps.inc(V.tensor_tensor(rw["nt"][:, g, :, :], scores_of(c)[:, :, 0:P],
                                                  ident[:, :].rearrange("p (o s) -> p o s", o=1).to_broadcast([P, 4, P]), ALU.add))
                    steps.wait()
                    for g in range(2):
                        c = 2 * p + g
                        V.tensor_tensor(dh(rw["tt"][:, c, :, :]), dh(rw["nt"][:, g, :, :]),
                                        bc(rw["lmask"][:, 0, :, :], 2), ALU.mult).then_inc(W["nt"], 1)
                    for lev in range(1, LEVELS):
                        for g in range(2):
                            dve.wait_ge(W["x_ps"], i * 24 + (p * 12 + (lev - 1) * 2 + g + 1))
                            V.tensor_tensor(dh(xb[:, g, :, :]), dh(ps[:, GB[g][0], :].rearrange("p (t s) -> p t s", t=4)),
                                            bc(rw["lmask"][:, lev, :, :], 2), ALU.mult).then_inc(W["x"], 1)
                sp = rw["sp"]
                for c in range(4):
                    dve.wait_ge(W["u_ps"], i * 4 + (c + 1))
                    V.tensor_copy(rw["u"][:, :, :], ps[:, 6, 0:4 * HD].rearrange("p (t s) -> p t s", t=4)).then_inc(W["u"], 1)
                    if c == 2:
                        dve.wait_ge(W["o_ps"], i * 2 + 1)
                        V.tensor_copy(rw["o"][:, :], ps[:, 2, 0:SEQ]).then_inc(W["o"], 1)
                        dve.wait_ge(W["o"], i * 2 + 1)
                    if c == 3:
                        dve.wait_ge(W["o_ps"], i * 2 + 2)
                        steps.link(V.tensor_tensor(rw["o"][:, P:SEQ], ps[:, 2, 0:P], rw["o"][:, P:SEQ], ALU.add))
                        V.tensor_tensor(rw["o"][:, 0:P], ps[:, 2, P:SEQ], rw["o"][:, 0:P], ALU.add).then_inc(W["o"], 1)
                    if c < 3:
                        dve.wait_ge(W["st_ps"], i * 3 + (c + 1))
                        src = ps[:, 3, 0:2 * HD].rearrange("p (d s) -> p d s", d=2)
                        if c:
                            steps.link(V.tensor_tensor(sp[:, :, :], src, sp[:, :, :], ALU.add))
                            src = sp[:, :, :]
                        for d in range(2):
                            ins = V.tensor_scalar(sp[:, d, :], src[:, d, :], rw["pm"][:, d, c, 0:1], None, ALU.mult)
                        ins.then_inc(W["sp"], 1)
                        dve.wait_ge(W["sp"], i * 3 + (c + 1))
                steps.link(V.tensor_tensor(t12[:, 1, 0:SEQ], rw["kd"][:, 0, SEQ:TOK], rw["kd"][:, 1, SEQ:TOK], ALU.add))
                V.scalar_tensor_tensor(out=t12[:, 1, 0:SEQ], in0=t12[:, 1, 0:SEQ], scalar=cur[:, C_RK:C_RK + 1],
                                       in1=rw["r"][:, :], op0=ALU.mult, op1=ALU.mult).then_inc(W["pr"], 1)
                dve.wait_ge(W["mean_ps"], i + 1)
                dve.wait_ge(W["o"], i * 2 + 2)
                V.scalar_tensor_tensor(out=rw["o"][:, :], in0=ps[:, 6, 0:SEQ], scalar=-1.0 / HD, in1=rw["o"][:, :],
                                       op0=ALU.mult, op1=ALU.add).then_inc(W["om"], 1)
                dve.wait_ge(W["bon_ps"], i + 1)
                steps.inc(V.tensor_tensor(t12[:, 1, SEQ:TOK], ps[:, 6, SEQ:TOK], rw["v"][:, SEQ:TOK], ALU.mult))
                dve.wait_ge(W["std"], i + 1)
                steps.link(V.reciprocal(t12[:, 1, 0:SEQ], t12[:, 0, SEQ:TOK]))
                steps.link(V.tensor_tensor(t12[:, 0, 0:SEQ], rw["o"][:, :], t12[:, 1, 0:SEQ], ALU.mult))
                steps.link(V.tensor_scalar(t12[:, 0, 0:SEQ], t12[:, 0, 0:SEQ], cur[:, C_GW:C_GW + 1], cur[:, C_GB:C_GB + 1], ALU.mult, ALU.add))
                steps.link(V.tensor_tensor(t12[:, 0, 0:SEQ], t12[:, 0, 0:SEQ], t12[:, 1, SEQ:TOK], ALU.add))
                dve.wait_ge(W["g_ps"], i + 2)
                V.tensor_tensor(yT[:, bass.ds(i + HEADS, 1), :], t12[:, 0:1, 0:SEQ], ps[:, 7:8, SEQ:TOK], ALU.mult).then_inc(W["y"], 1)
            steps.leave(HEADS)

        def rwkv_pe(pe):
            W = rws
            stage_end(pe, 2)
            pe.wait_ge(W["cst2"], 3)
            pe.wait_ge(W["init"], 2)
            pe.wait_ge(W["cst"], 64)
            R = rw
            half = lambda h: slice(h * HD, (h + 1) * HD)
            xb = R["t12"][:, :, :].rearrange("p g (t s) -> p g t s", t=4)
            with pe.Fori(0, HEADS) as i:
                ada = iter([(j, c) for j in range(1, ADA_R) for c in range(NCH)])

                def ada_gap():
                    j, c = next(ada)
                    q = i * ADA_R + (Q_RW + j)
                    pe_ada_chunk(pe, q, q + MIX_M, c)
                    if j > 1 and c == 0:
                        sum_of(j - 1)

                def sum_of(j):
                    loads = i + (ADA_A // 2 + HEADS + 1, ADA_A // 2 + 1, 1, 1)[j]
                    pe_ada_sum(pe, i * ADA_R + (Q_RW + j), j, loads)

                pe.wait_ge(W["in"], i * 96 + 96)
                for d in range(2):
                    pe.matmul(ps[:, 1 + d, :], R["aup"][half(d), :], R["al"][half(d), :], start=True, stop=True).then_inc(W["a_ps"], 1)
                pe.wait_ge(W["y"], i + 1)
                for d in range(2):
                    b = (3, 6)[d]
                    for t in range(4):
                        o = ps[:, b, t * P:(t + 1) * P]
                        pe.matmul(o, R["th"][half(d), t * P:(t + 1) * P], R["wup"][half(d), :], start=True, stop=False)
                        mm = pe.matmul(o, ones[0:1, 0:P], R["w0"][0:1, d, :], start=False, stop=True)
                    mm.then_inc(W["z_ps"], 1)
                pe.wait_ge(W["sq"], i + 1)
                pe.matmul(ps[:, 0, :], R["blk"][:, :], R["t12"][:, 0, :], start=True, stop=True).then_inc(W["nrm_ps"], 1)
                for n in range(4):
                    d, pr, b = n // 2, n % 2, (0, 7, 1, 2)[n]
                    pe.wait_ge(W["lw"], i * 2 + (d + 1))
                    if n == 0:
                        pe.wait_ge(W["nrm"], i + 1)
                        pe.wait_ge(W["a"], i * 2 + 2)
                    for e in range(2):
                        mm = pe.matmul(ps[:, b, e * (P + 1):(e + 1) * (P + 1)], R["lw"][:, d, 2 * pr + e, :], R["tri"][:, d, :],
                                       start=True, stop=True)
                    mm.then_inc(W["cum_ps"], 1)
                pe.wait_ge(W["v"], i + 2)
                for n, (b, src) in enumerate([(3, R["v"]), (6, (R["kh"], 0)), (7, (R["kh"], 1)), (0, (R["bh"], 0)), (1, (R["bh"], 1))]):
                    if n == 1:
                        for c in range(NCH):
                            pe_ada_chunk(pe, i * ADA_R + Q_RW, i * ADA_R + (Q_RW + MIX_M), c)
                        pe.wait_ge(W["prod"], i + 1)
                        pe.wait_ge(W["cum"], i * 4 + 4)
                    for t in range(4):
                        s = src[:, t * P:(t + 1) * P] if n == 0 else src[0][:, src[1], t, :]
                        tr = pe.transpose(ps[:, b, t * P:(t + 1) * P], s, ident[:, :])
                    tr.then_inc(W["tr_ps"], 1)
                sum_of(0)
                pe.wait_ge(W["tr"], i * 5 + 5)
                n = 0
                for c in range(4):
                    for inst in range(4):
                        d, h = inst // 2, inst % 2
                        t, b, w_ = SCAN[d][c], SCB[n % 6], (2 * P if LAT[c] else P)
                        if n >= 6:
                            pe.wait_ge(W["sc"], i * 16 + (n - 5))
                        rhs = R["kx"][half(h), d, t, :, :] if LAT[c] else R["kx"][half(h), d, t, 0, :]
                        pe.matmul(ps[:, b, 0:w_], R["bh"][half(h), d, t, :], rhs, start=True, stop=True)
                        pe.matmul(ps[:, b, w_:2 * w_], R["kh"][half(h), d, t, :], rhs, start=True, stop=True).then_inc(W["sc_ps"], 1)
                        n += 1
                def next_x(p, lev, g):
                    pe.wait_ge(W["t"], i * 24 + (p * 12 + (lev - 1) * 2 + g + 1))
                    for inst in range(4):
                        mm = pe.matmul(ps[:, GB[g][0], inst * P:(inst + 1) * P], R["nt"][:, g, inst, :], R["tb"][:, g, inst, :],
                                       start=True, stop=True)
                    mm.then_inc(W["x_ps"], 1)

                for p in range(2):
                    for g in range(2):
                        pe.wait_ge(W["nt"], i * 4 + (2 * p + g + 1))
                        if g == 0:
                            pe.wait_ge(W["sc"], i * 16 + 16)
                        if p:
                            pe.wait_ge(W["tt"], i * 24 + (10 + g + 1))
                        for inst in range(4):
                            tr = pe.transpose(ps[:, GB[g][1], inst * P:(inst + 1) * P], R["tt"][:, 2 * p + g, inst, :], ident[:, :])
                        tr.then_inc(W["t_ps"], 1)
                    for g in range(2):
                        next_x(p, 1, g)
                    for lev in range(1, LEVELS):
                        for g in range(2):
                            pe.wait_ge(W["x"], i * 24 + (p * 12 + (lev - 1) * 2 + g + 1))
                            if lev > 1:
                                pe.wait_ge(W["tt"], i * 24 + (p * 12 + (lev - 2) * 2 + g + 1))
                            last = lev == LEVELS - 1
                            for inst in range(4):
                                tt, x = R["tt"][:, 2 * p + g, inst, :], xb[:, g, inst, :]
                                l, r = (x, tt) if last else (tt, x)
                                mm = pe.matmul(ps[:, GB[g][2 if last else 1], inst * P:(inst + 1) * P], l, r, start=True, stop=True)
                            mm.then_inc(W["tt_ps"] if last else W["t_ps"], 1)
                        if last:
                            continue
                        for g in range(2):
                            pe.wait_ge(W["t"], i * 24 + (p * 12 + lev * 2 + g + 1))
                            for inst in range(4):
                                tr = pe.transpose(ps[:, GB[g][2], inst * P:(inst + 1) * P], R["tb"][:, g, inst, :], ident[:, :])
                            tr.then_inc(W["tt_ps"], 1)
                            next_x(p, lev + 1, g)
                pe.wait_ge(W["tt"], i * 24 + 24)
                for c in range(4):
                    if c:
                        pe.wait_ge(W["sp"], i * 3 + c)
                    for inst in range(4):
                        d, h = inst // 2, inst % 2
                        t, o = SCAN[d][c], ps[:, RHB[h], d * HD:(d + 1) * HD]
                        mm = pe.matmul(o, bt(c, inst), R["vt"][:, t, half(h)], start=True, stop=(c == 0))
                        if c:
                            mm = pe.matmul(o, R["kx"][half(h), d, t, 0, :], R["sp"][half(h), d, :], start=False, stop=True)
                    mm.then_inc(W["rh_ps"], 1)
                    ada_gap()
                    pe.wait_ge(W["rh"], i * 4 + (c + 1))
                    for inst in range(4):
                        mm = pe.matmul(ps[:, 6, inst * HD:(inst + 1) * HD], R["tt"][:, c, inst, :], R["rh"][:, inst, :], start=True, stop=True)
                    mm.then_inc(W["u_ps"], 1)
                    ada_gap()
                    pe.wait_ge(W["u"], i * 4 + (c + 1))
                    if LAT[c]:
                        if c == 3:
                            pe.wait_ge(W["o"], i * 2 + 1)
                        for inst in range(4):
                            d, h = inst // 2, inst % 2
                            t, o = SCAN[d][c], ps[half(h), 2, d * P:(d + 1) * P]
                            pe.matmul(o, R["vt"][:, t, half(h)], R["scl"][:, c - 2, inst, 3 * P:4 * P], start=True, stop=False)
                            pe.matmul(o, R["sp"][half(h), d, :], R["kx"][half(h), d, t, 1, :], start=False, stop=False)
                            mm = pe.matmul(o, R["u"][:, inst, :], R["scl"][:, c - 2, inst, P:2 * P], start=False, stop=True)
                        mm.then_inc(W["o_ps"], 1)
                    if c < 3:
                        for inst in range(4):
                            d, h = inst // 2, inst % 2
                            t, o = SCAN[d][c], ps[half(h), 3, d * HD:(d + 1) * HD]
                            pe.matmul(o, R["kht"][:, d, t, half(h)], R["vt"][:, t, half(h)], start=True, stop=False)
                            mm = pe.matmul(o, R["bht"][:, d, t, half(h)], R["u"][:, inst, :], start=False, stop=True)
                        mm.then_inc(W["st_ps"], 1)
                    ada_gap()
                pe.wait_ge(W["pr"], i + 1)
                pe.matmul(ps[:, 6, SEQ:TOK], R["blk"][:, :], R["t12"][:, 1, 0:SEQ], start=True, stop=True).then_inc(W["bon_ps"], 1)
                pe.wait_ge(W["gin"], i * 32 + 32)
                pe.matmul(ps[:, 7, SEQ:TOK], R["gup"][:, 0, :], R["sg"][:, 0, :], start=True, stop=False)
                pe.matmul(ps[:, 7, SEQ:TOK], R["gup"][0:32, 1, :], R["sg"][0:32, 1, :], start=False, stop=True).then_inc(W["g_ps"], 1)
                sum_of(ADA_R - 1)
                pe.wait_ge(W["o"], i * 2 + 2)
                pe.matmul(ps[:, 6, 0:SEQ], R["blk"][:, :], R["o"][:, :], start=True, stop=True).then_inc(W["mean_ps"], 1)
                pe.wait_ge(W["sqo"], i + 1)
                pe.matmul(ps[:, 7, 0:SEQ], R["blk"][:, :], R["t12"][:, 0, 0:SEQ], start=True, stop=True).then_inc(W["var_ps"], 1)

        M_OUT, M_MLP0 = MIX_M, MIX_M + 4
        M_PW1 = M_MLP0 + 32
        M_PW2 = M_PW1 + 8
        M_MLP1 = M_PW2 + 4
        B_OFF = Q_ALL
        Q4 = D_FF // D
        ysp_hi, ysp_lo, h_in = sem("ysp_hi"), sem("ysp_lo"), sem("h_in")
        gate_in, line_in = sem("gate_in"), sem("line_in")
        res_ps, res_add = sem("res_ps"), sem("res_add")
        act_ps = sem("act_ps")
        sq_ok, hact_hi, hact_lo = sem("sq_ok"), sem("hact_hi"), sem("hact_lo")
        glu_ok, conv_ok, mean_ps, cen_ok, csq_ok, var_ps2, cstd_ok = (sem(n) for n in (
            "glu_ok", "conv_ok", "mean_ps", "cen_ok", "csq_ok", "var_ps2", "cstd_ok"))
        un_ok, sgm_ok, sil_ok, un_hi, un_lo = (sem(n) for n in ("un_ok", "sgm_ok", "sil_ok", "un_hi", "un_lo"))
        diag_a, diag_p, diag_used = sem("diag_a"), sem("diag_p"), sem("diag_used")
        TR0, TR1, TR2 = 16, 24, 32
        quad = lambda x: x.rearrange("p a (b t) -> p (a b) t", t=SEQ)

        def token_groups(u, hi, lo):
            return [(False, (0, NB), lambda k, t=t: hi[:, k, t * P:(t + 1) * P], lambda k, t=t: lo[:, k, t * P:(t + 1) * P],
                     ps[:, 2 * u + t, :], True) for t in range(2)]

        def feature_groups(u, hi, lo):
            return [(True, (j * P, (j + 1) * P), lambda k: hi[:, k, :], lambda k: lo[:, k, :],
                     ps[:, 2 * u + j // 2, (j % 2) * SEQ:(j % 2 + 1) * SEQ], j % 2 == 0) for j in range(4)]

        def sync_rest(sp):
            src = lambda m: ("product", m - 1)
            for e in range(4):
                send(sp, weight_src(w["out"], e * NB), NB, src(M_OUT + e) if e else ("ada", Q_ALL - 1))

            def mlp(l, m0):
                with sp.Fori(0, Q4) as i:
                    for k in range(4):
                        send(sp, weight_src(a["mlp_w1"][l], i * D + k * NB), NB, src(i * 8 + (m0 + k)))
                    for k in range(4):
                        send(sp, weight_src(a["mlp_w2"][l], k * NB, NB, i * D), NB, src(i * 8 + (m0 + 4 + k)))

            mlp(0, M_MLP0)
            for n in range(8):
                send(sp, weight_src(w["pw1"], n // 2 * NB + n % 2 * D), NB, src(M_PW1 + n))
            for n in range(4):
                send(sp, weight_src(w["pw2"], n * NB), NB, src(M_PW2 + n))
            mlp(1, M_MLP1)
            for k in range(4):
                sp.wait_ge(res_add, 36 + k + 1)
                sp.dma_start(out[0, :, k * NB:(k + 1) * NB].rearrange("(t p) n -> p t n", p=P), hbuf[:, :, k * NB:(k + 1) * NB]).then_inc(out_done, 16)
            sp.wait_ge(out_done, 64)

        def pool_rest(pool):
            stage_end(pool, 3)

            def load_gate(l, c):
                pool.dma_start(gate[:, :], mod_d[l, 0:1, c * D:(c + 1) * D].to_broadcast([P, D])).then_inc(gate_in, 16)

            pool.wait_ge(ada_st, 16 * Q_ALL)
            load_gate(0, 2)
            pool.dma_start(mrow[0:32, :], rows_of(mod_d[0, 0, 3 * D:5 * D])).then_inc(mrow_in, 16)
            pool.dma_start(mrow[32:64, :], rows_of(mod_d[1, 0, 0:2 * D])).then_inc(mrow_in, 16)
            pool.dma_start(mrow[64:96, :], rows_of(mod_d[1, 0, 3 * D:5 * D])).then_inc(mrow_in, 16)
            pool.dma_start(line[0:1, :, :], a["conv_pw2_b"].rearrange("a (b n) -> a b n", n=NB)).then_inc(line_in, 16)
            pool.wait_ge(ysp_hi, 4)
            pool.wait_ge(ysp_lo, 4)
            pool.dma_start(hbuf[:, :, :], a["x"][0].rearrange("(t p) d -> p t d", p=P)).then_inc(h_in, 16)
            for n, (l, c) in ((4, (0, 5)), (20, (1, 2)), (24, (1, 5))):
                pool.wait_ge(res_add, n)
                load_gate(l, c)
                if n == 20:
                    pool.wait_ge(lo_done, 4 * (M_PW1 + 1))
                    for m in range(M_PW1 + 1, M_PW1 + 9):
                        for ch in range(NCH):
                            pool.wait_ge(hi_done, 4 * m + ch + 1)
                            nc.gpsimd.tensor_tensor(split_lo[:, ch, :, :], raw[:, ch, :, :], split_hi[:, ch, :, :],
                                                    ALU.subtract).then_inc(lo_done, 1)
                    pool.wait_ge(pe_chunk, 4 * (M_PW1 + 8))
                    for t in range(TAPS):
                        if t % 3 == 2:
                            continue
                        if t >= 8:
                            pool.wait_ge(diag_used, t - 7)
                        nc.gpsimd.tensor_tensor(diag[:, t % 8, :, :], ident[:, :].rearrange("p (o s) -> p o s", o=1).to_broadcast([P, PE_F, P]),
                                                dwc[:, KT - PE_F:KT, t:t + 1].to_broadcast([P, PE_F, P]), ALU.mult).then_inc(diag_p, 1)

        def act_rest(act, steps):
            stage_end(act, 3)
            for c in range(4):
                nc.scalar.activation(xa_hi[:, 4 * c:4 * c + 4, :], yT[:, 4 * c:4 * c + 4, :], ACT.Copy).then_inc(ysp_hi, 1)
            act_split(act, M_OUT, M_OUT + B_OFF)
            for e in range(4):
                act_split(act, M_OUT + e + 1, M_OUT + e + 1 + B_OFF)

            def norm(q, tr0):
                act.wait_ge(res_add, (4, 20, 24)[q - 1])
                act_stats(act, q, hbuf, xn2, 2)
                act_high(act, tr0, 2, lambda i: xa_hi[:, 2 * i:2 * i + 2, :])

            def mlp_quarter(i, m0, abase, rbase, last):
                for k in range(8):
                    m = i * 8 + (m0 + k)
                    if not (last and k == 7):
                        act_split(act, m + 1, m + (1 + B_OFF))
                    if k < 4:
                        act.wait_ge(pe_chunk, m * 4 + 4)
                        if k == 0:
                            act.wait_ge(res_add, i * 4 + rbase)
                        else:
                            act.wait_ge(hact_lo, i * 4 + (abase[1] + k))
                        nc.scalar.activation(tmpa[:, :, :], ps[:, 2 * (k % 2):2 * (k % 2) + 2, :], ACT.Relu).then_inc(act_ps, 1)
                        act.wait_ge(sq_ok, i * 4 + (abase[1] + k + 1))
                        nc.scalar.activation(hT_hi[:, 4 * k:4 * k + 4, :], quad(tmpa[:, :, :]), ACT.Copy).then_inc(hact_hi, 1)

            norm(1, TR0)
            with act.Fori(0, Q4) as i:
                mlp_quarter(i, M_MLP0, (0, 0), 4, False)
            norm(2, TR1)
            for n in range(8):
                m, b = M_PW1 + n, n // 2
                act_split(act, m + 1, m + 1 + B_OFF)
                act.wait_ge(pe_chunk, 4 * m + 4)
                if n % 2 == 0 and b:
                    act.wait_ge(glu_ok, b)
                for j in range(4):
                    src = ps[:, 2 * (n % 2) + j // 2, (j % 2) * SEQ:(j % 2 + 1) * SEQ]
                    bias = col_of("pw1b", (n % 2) * KT + 4 * b + j)
                    if n % 2 == 0:
                        ins = nc.scalar.activation(quad(tmpa[:, :, :])[:, j, :], src, ACT.Identity, bias=bias)
                    else:
                        ins = nc.scalar.activation(gpad[:, 4 * b + j, PADW:PADW + SEQ], src, ACT.Sigmoid, bias=bias)
                ins.then_inc(act_ps, 1)
            act.wait_ge(pe_chunk, 4 * (M_PW1 + 8))
            for t in range(2, TAPS, 3):
                if t >= 8:
                    act.wait_ge(diag_used, t - 7)
                for j in range(PE_F):
                    ins = nc.scalar.activation(diag[:, t % 8, j, :], ident[:, :], ACT.Copy, scale=dwc[:, KT - PE_F + j, t:t + 1])
                ins.then_inc(diag_a, 1)
            for p in range(4):
                act.wait_ge(cen_ok, p + 1)
                nc.scalar.activation(gpad[:, 4 * p:4 * p + 4, 0:SEQ], cu[:, 4 * p:4 * p + 4, :], ACT.Square).then_inc(csq_ok, 1)
            act.wait_ge(var_ps2, 1)
            nc.scalar.activation(tmpa[:, 0, 0:SEQ], ps[:, 7, 0:SEQ], ACT.Sqrt, scale=1.0 / D, bias=epsc[:, 0:1]).then_inc(cstd_ok, 1)
            for p in range(5):
                if p < 4:
                    act.wait_ge(un_ok, p + 1)
                    nc.scalar.activation(gpad[:, 4 * p:4 * p + 4, 0:SEQ], cu[:, 4 * p:4 * p + 4, :], ACT.Sigmoid).then_inc(sgm_ok, 1)
                if p:
                    act.wait_ge(sil_ok, p)
                    nc.scalar.activation(xa_hi[:, 4 * p - 4:4 * p, :], cu[:, 4 * p - 4:4 * p, :], ACT.Copy).then_inc(un_hi, 1)
            for n in range(4):
                act_split(act, M_PW2 + n + 1, M_PW2 + n + 1 + B_OFF)
            norm(3, TR2)
            with act.Fori(0, Q4 - 1) as i:
                mlp_quarter(i, M_MLP1, (24, 16), 24, False)
            mlp_quarter(Q4 - 1, M_MLP1, (24, 16), 24, True)

        def dve_rest(dve, steps):
            V = nc.vector
            stage_end(dve, 3)
            for c in range(4):
                dve.wait_ge(ysp_hi, c + 1)
                V.tensor_tensor(xa_lo[:, 4 * c:4 * c + 4, :], yT[:, 4 * c:4 * c + 4, :], xa_hi[:, 4 * c:4 * c + 4, :],
                                ALU.subtract).then_inc(ysp_lo, 1)
            dve.wait_ge(mt_ps, 2)
            steps.link(V.tensor_copy(mcol[:, 0:96], ps[:, 6, 0:96]))
            for n, (name, o) in ((2, ("n2g0", 0)), (3, ("n1g1", 32)), (4, ("n2g1", 64))):
                steps.inc(V.scalar_tensor_tensor(out=gcol[:, n, :], in0=mcol[:, o + 16:o + 32], scalar=1.0,
                                                 in1=col_of(name, 0, KT), op0=ALU.add, op1=ALU.mult))
            steps.wait()
            dve.wait_ge(h_in, 16)

            def residual(m, k):
                dve.wait_ge(pe_chunk, m * 4 + 4)
                cols = slice(k * NB, (k + 1) * NB)
                gb = gate[:, cols].rearrange("p (o n) -> p o n", o=1).to_broadcast([P, 2, NB])
                V.tensor_tensor(tmpa[:, :, :], ps[:, 2 * (k % 2):2 * (k % 2) + 2, :], gb, ALU.mult).then_inc(res_ps, 1)

            def add(k, count):
                cols = slice(k * NB, (k + 1) * NB)
                dve.wait_ge(res_ps, count)
                V.tensor_tensor(hbuf[:, :, cols], hbuf[:, :, cols], tmpa[:, :, :], ALU.add).then_inc(res_add, 1)
                dve.wait_ge(res_add, count)

            def norm(q, tr0, o):
                dve_scale(dve, q, steps, hbuf, xn2, 2)
                dve_modulate(dve, tr0, 2, [(gcol[:, q + 1, :], mcol[:, o:o + 16])],
                             lambda i: xa_hi[:, 2 * i:2 * i + 2, :], lambda i: xa_lo[:, 2 * i:2 * i + 2, :])

            def mlp_quarter(i, m0, abase, rbase, last):
                for k in range(8):
                    m = i * 8 + (m0 + k)
                    if not (last and k == 7):
                        dve_split(dve, m + 1, m + (1 + B_OFF))
                    if k < 4:
                        dve.wait_ge(act_ps, i * 4 + (abase[0] + k + 1))
                        V.tensor_tensor(tmpa[:, :, :], tmpa[:, :, :], tmpa[:, :, :], ALU.mult).then_inc(sq_ok, 1)
                        dve.wait_ge(hact_hi, i * 4 + (abase[1] + k + 1))
                        V.tensor_tensor(hT_lo[:, 4 * k:4 * k + 4, :], quad(tmpa[:, :, :]), hT_hi[:, 4 * k:4 * k + 4, :],
                                        ALU.subtract).then_inc(hact_lo, 1)
                    else:
                        if k == 4:
                            dve.wait_ge(hact_lo, i * 4 + (abase[1] + 4))
                        residual(m, k - 4)
                        add(k - 4, i * 4 + (rbase + k - 3))

            dve_split(dve, M_OUT, M_OUT + B_OFF)
            dve.wait_ge(gate_in, 16)
            for e in range(4):
                dve_split(dve, M_OUT + e + 1, M_OUT + e + 1 + B_OFF)
                residual(M_OUT + e, e)
                add(e, e + 1)
            norm(1, TR0, 0)
            dve.wait_ge(gate_in, 32)
            with dve.Fori(0, Q4) as i:
                mlp_quarter(i, M_MLP0, (0, 0), 4, False)
            norm(2, TR1, 32)
            steps.inc(V.memset(gpad[:, :, 0:PADW], 0.0))
            steps.link(V.memset(gpad[:, :, PADW + SEQ:], 0.0))

            done = {}

            def tap(f, t):
                x, wt = gpad[:, f, t:t + SEQ], dwc[:, f, t:t + 1]
                if t == 0:
                    ins = V.tensor_scalar(cu[:, f, :], x, wt, col_of("dwb", f), ALU.mult, ALU.add)
                else:
                    dve.wait_ge(steps.sem, done[f])
                    ins = V.scalar_tensor_tensor(out=cu[:, f, :], in0=x, scalar=wt, in1=cu[:, f, :], op0=ALU.mult, op1=ALU.add)
                steps.inc(ins)
                done[f] = steps.base + steps.n

            def convolved():
                steps.wait()
                V.tensor_copy(small[:, 16:17], small[:, 17:18]).then_inc(conv_ok, 1)

            def gate_block(b):
                dve.wait_ge(act_ps, 16 + 2 * b + 2)
                g = gpad[:, 4 * b:4 * b + 4, PADW:PADW + SEQ]
                V.tensor_tensor(g, g, quad(tmpa[:, :, :]), ALU.mult).then_inc(glu_ok, 1)
                dve.wait_ge(glu_ok, b + 1)

            for b in range(3):
                gate_block(b)
                for t in range(TAPS if b < 2 else TAPS // 2 + 1):
                    for f in range(4 * b, 4 * b + 4):
                        tap(f, t)
                if b < 2:
                    convolved()
            gate_block(3)
            for n, t in enumerate(range(TAPS // 2 + 1, TAPS)):
                for f, k in ((8, t), (12, 2 * n), (9, t), (10, t), (12, 2 * n + 1), (11, t)):
                    tap(f, k)
            tap(12, TAPS - 1)
            convolved()
            dve.wait_ge(diag_used, TAPS)
            for j in range(PE_F):
                f = KT - PE_F + j
                steps.inc(V.tensor_scalar(cu[:, f, :], ps[:, j // 2, (j % 2) * SEQ:(j % 2 + 1) * SEQ], col_of("dwb", f), None, ALU.add))
            convolved()
            bcast = lambda x: x.rearrange("p (o t) -> p o t", o=1).to_broadcast([P, 4, SEQ])
            dve.wait_ge(mean_ps, 1)
            for p in range(4):
                c4 = cu[:, 4 * p:4 * p + 4, :]
                V.scalar_tensor_tensor(out=c4, in0=bcast(ps[:, 6, 0:SEQ]), scalar=-1.0 / D, in1=c4, op0=ALU.mult, op1=ALU.add).then_inc(cen_ok, 1)
            dve.wait_ge(cstd_ok, 1)
            steps.link(V.reciprocal(tmpa[:, 0, SEQ:2 * SEQ], tmpa[:, 0, 0:SEQ]))
            dve.wait_ge(cen_ok, 4)
            group = lambda p: cu[:, 4 * p:4 * p + 4, :]
            for p in range(6):
                if p < 4:
                    steps.link(V.tensor_tensor(group(p), group(p), bcast(tmpa[:, 0, SEQ:2 * SEQ]), ALU.mult))
                    for f in range(4 * p, 4 * p + 4):
                        ins = V.tensor_scalar(cu[:, f, :], cu[:, f, :], col_of("lng", f), col_of("lnb", f), ALU.mult, ALU.add)
                    ins.then_inc(un_ok, 1)
                if 1 <= p < 5:
                    dve.wait_ge(un_ok, p)
                    dve.wait_ge(sgm_ok, p)
                    V.tensor_tensor(group(p - 1), group(p - 1), gpad[:, 4 * p - 4:4 * p, 0:SEQ], ALU.mult).then_inc(sil_ok, 1)
                if p >= 2:
                    dve.wait_ge(un_hi, p - 1)
                    V.tensor_tensor(xa_lo[:, 4 * p - 8:4 * p - 4, :], group(p - 2), xa_hi[:, 4 * p - 8:4 * p - 4, :],
                                    ALU.subtract).then_inc(un_lo, 1)
            dve.wait_ge(gate_in, 48)
            for n in range(4):
                if n == 0:
                    dve.wait_ge(lo_done, 4 * (M_PW2 + 1))
                dve_split(dve, M_PW2 + n + 1, M_PW2 + n + 1 + B_OFF)
                residual(M_PW2 + n, n)
                add(n, 20 + n + 1)
            norm(3, TR2, 64)
            dve.wait_ge(gate_in, 64)
            with dve.Fori(0, Q4 - 1) as i:
                mlp_quarter(i, M_MLP1, (24, 16), 24, False)
            mlp_quarter(Q4 - 1, M_MLP1, (24, 16), 24, True)

        def pe_rest(pe):
            stage_end(pe, 3)
            pe.wait_ge(rws["y"], HEADS + 1)
            pe.wait_ge(mrow_in, 16 * 5)
            pe.transpose(ps[:, 6, 0:96], mrow[0:96, :], ident[0:96, 0:96]).then_inc(mt_ps, 1)

            def two(f):
                return lambda g: f() if g == 0 else None

            for e in range(4):
                def ready(c, e=e):
                    if e == 0:
                        pe.wait_ge(ysp_hi, c + 1)
                        pe.wait_ge(ysp_lo, c + 1)
                pe_product(pe, M_OUT + e, token_groups(e % 2, xa_hi, xa_lo), ready,
                           two(lambda e=e: pe.wait_ge(res_ps, e - 1)) if e >= 2 else None)

            def norm(q, tr0):
                pe.wait_ge(norm_xn, q + 1)
                pe.wait_ge(res_ps, (4, 20, 24)[q - 1])
                pe_transposes(pe, tr0, xn2, 2)

            def normed(tr0, c):
                pe.wait_ge(tr_hi, tr0 + 2 * c + 2)
                pe.wait_ge(tr_lo, tr0 + 2 * c + 2)

            def mlp(m0, abase, rbase, tr0):
                with pe.Fori(0, Q4) as i:
                    for k in range(4):
                        def free(k=k):
                            if k < 2:
                                pe.wait_ge(res_ps, i * 4 + (rbase - 1 + k))
                                pe.wait_ge(tr_ts, tr0 + 8)
                            else:
                                pe.wait_ge(act_ps, i * 4 + (abase[0] + k - 1))
                        pe_product(pe, i * 8 + (m0 + k), feature_groups(k % 2, xa_hi, xa_lo),
                                   (lambda c: normed(tr0, c)) if k == 0 else None, two(free))
                    for k in range(4):
                        def free(k=k):
                            if k < 2:
                                pe.wait_ge(act_ps, i * 4 + (abase[0] + k + 3))
                            else:
                                pe.wait_ge(res_ps, i * 4 + (rbase + k - 1))

                        def ready(c):
                            pe.wait_ge(hact_hi, i * 4 + (abase[1] + c + 1))
                            pe.wait_ge(hact_lo, i * 4 + (abase[1] + c + 1))
                        pe_product(pe, i * 8 + (m0 + 4 + k), token_groups(k % 2, hT_hi, hT_lo), ready if k == 0 else None, two(free))

            norm(1, TR0)
            mlp(M_MLP0, (0, 0), 4, TR0)
            norm(2, TR1)
            for n in range(8):
                def free(n=n):
                    if n < 2:
                        pe.wait_ge(tr_ts, TR1 + 8)
                    else:
                        pe.wait_ge(act_ps, 16 + n - 1)
                pe_product(pe, M_PW1 + n, feature_groups(n % 2, xa_hi, xa_lo), (lambda c: normed(TR1, c)) if n == 0 else None, two(free))
            pe.wait_ge(glu_ok, 4)
            pe.wait_ge(act_ps, 24)
            for t in range(TAPS):
                if t % 3 == 2:
                    pe.wait_ge(diag_a, (t + 1) // 3)
                else:
                    pe.wait_ge(diag_p, t + 1 - (t + 1) // 3)
                for j in range(PE_F):
                    mm = pe.matmul(ps[:, j // 2, (j % 2) * SEQ:(j % 2 + 1) * SEQ], diag[:, t % 8, j, :], gpad[:, KT - PE_F + j, t:t + SEQ],
                                   start=(t == 0 and j % 2 == 0), stop=(t == TAPS - 1), skip_group_check=True)
                mm.then_inc(diag_used, 1)
            for b in range(4):
                pe.wait_ge(conv_ok, b + 1)
                for f in range(4 * b, 4 * b + 4):
                    mm = pe.matmul(ps[:, 6, 0:SEQ], ones[:, :], cu[:, f, :], start=(f == 0), stop=(f == KT - 1))
            mm.then_inc(mean_ps, 1)
            for b in range(4):
                pe.wait_ge(csq_ok, b + 1)
                for f in range(4 * b, 4 * b + 4):
                    mm = pe.matmul(ps[:, 7, 0:SEQ], ones[:, :], gpad[:, f, 0:SEQ], start=(f == 0), stop=(f == KT - 1))
            mm.then_inc(var_ps2, 1)
            pe.wait_ge(line_in, 16)
            for n in range(4):
                def ready(c, n=n):
                    if c == 0:
                        if n >= 2:
                            pe.wait_ge(res_ps, 20 + n - 1)
                        else:
                            pe.wait_ge(act_ps, 24)
                        for t in range(2):
                            pe.matmul(ps[:, 2 * (n % 2) + t, :], ones[0:1, 0:P], line[0:1, n, :], start=True, stop=False, skip_group_check=True)
                    if n == 0:
                        pe.wait_ge(un_hi, c + 1)
                        pe.wait_ge(un_lo, c + 1)
                groups = [g[:5] + (False,) for g in token_groups(n % 2, xa_hi, xa_lo)]
                pe_product(pe, M_PW2 + n, groups, ready)
            norm(3, TR2)
            mlp(M_MLP1, (24, 16), 24, TR2)

        block = top.enter_context(nc.Block())

        @block.sync
        def _(sp):
            sp.dma_start(cvec[:, 0, :], a["c"].rearrange("a (p k) -> p (a k)", k=KT)).then_inc(cv_in, 16)
            sp.dma_start(cvec[:, 1, :], a["c_ctx"].rearrange("(p k) -> p k", k=KT)).then_inc(cv_in, 16)
            sp.dma_start(ident[:, :], a["ident"]).then_inc(cst_in, 16)
            sp.dma_start(sel[:, :], a["sel"]).then_inc(cst_in, 16)
            sp.dma_start(x4[:, 0:2, :], a["ctx"][0].rearrange("(t p) d -> p t d", p=P)).then_inc(x_in, 16)
            sp.dma_start(x4[:, 2:4, :], a["x"][0].rearrange("(t p) d -> p t d", p=P)).then_inc(x_in, 16)
            for q in range(ADA_A):
                send_ada(sp, 0, q * NB, q, q % 2, ("ada", q - 1) if q else None)
            for m in range(MIX_M):
                n = min(NB, IN_COLS - m * NB)
                send(sp, weight_src(w["in"], m * NB, n), n, ("product", m - 1) if m else ("ada", ADA_A - 1))
            sp.wait_ge(hi_done, 4 * MIX_M)
            sp.wait_ge(lo_done, 4 * MIX_M)
            sp.wait_ge(at_qk_in, 32)
            with sp.Fori(0, HEADS) as i:
                q = i + Q_AT
                send_ada(sp, 0, i * NB + Q_AT * NB, q, 0, ("ada", q - 1))
            sp.wait_ge(rws["in"], 96)
            with sp.Fori(0, HEADS) as i:
                for j in range(ADA_R):
                    q = i * ADA_R + (Q_RW + j)
                    send_ada(sp, *rwkv_ada(i, j), q, j, ("ada", q - 1))
            sync_rest(sp)

        @block.gpsimd
        def _(pool):
            pool.wait_ge(init_done, 1)
            rows = [(0, "n1g0", a["norm1_g"][0]), (0, "n1g1", a["norm1_g"][1]), (0, "n2g0", a["norm2_g"][0]),
                    (0, "n2g1", a["norm2_g"][1]), (0, "dwb", a["conv_dw_b"][0]), (0, "lng", a["conv_ln_g"][0]),
                    (0, "lnb", a["conv_ln_b"][0]), (1, "pw1b", a["conv_pw1_b"][0]),
                    (1, "mu", a["shift_mu"][0, 0:27 * P]), (1, "a0", a["iclr_a0"][0].rearrange("d n -> (d n)")),
                    (1, "kk", a["k_k"][0]), (1, "ka", a["k_a"][0]), (1, "rk", a["r_k"][0].rearrange("h n -> (h n)")),
                    (1, "gnw", a["gn_w"][0]), (1, "gnb", a["gn_b"][0])]
            for t, name, v in rows:
                r0 = (P0 if t == 0 else P1)[name]
                pool.dma_start(prow[t][r0:r0 + v.shape[0] // P, :], rows_of(v)).then_inc(prow_in, 16)
            pool.dma_start(prow[1][P1["mu"] + 27:P1["mu"] + 28, 0:32], a["shift_mu"][0:1, 27 * P:B_COLS]).then_inc(prow_in, 16)
            pool.dma_start(dwr, a["conv_dw_w"][0]).then_inc(prow_in, 16)
            pool.wait_ge(ada_st, 16 * ADA_A)
            pool.dma_start(mrow[0:32, :], rows_of(mod_d[0, 0, 0:2 * D])).then_inc(mrow_in, 16)
            pool.dma_start(mrow[32:64, :], rows_of(mod_d[0, 1, 0:2 * D])).then_inc(mrow_in, 16)
            for b in range(4):
                pool.wait_ge(mix_st[b], 16 * stored(MIX_M - 1, b))
            stage_end(pool, 1)
            with pool.Fori(0, HEADS) as i:
                pool.wait_ge(at_qkr, i * 2 + 2)
                pool.sem_inc(pool_go, 1)
                pool.dma_start(at["qk"][:, 0:4, :], qkv_d[:, bass.ds(i * P + AW, P)].rearrange("(t p) n -> p t n", p=P)).then_inc(at_qk_in, 16)
                pool.dma_start(at["qk"][:, 4:6, :], qkv_d[SEQ:TOK, bass.ds(i * P, P)].rearrange("(t p) n -> p t n", p=P)).then_inc(at_qk_in, 16)
                pool.wait_ge(at_o, i + 1)
                pool.sem_inc(pool_go, 1)
                pool.dma_start(at["v"][:, :, :], qkv_d[:, bass.ds(i * P + 2 * AW, P)].rearrange("(t p) n -> p t n", p=P)).then_inc(at_v_in, 16)
            rwkv_pool(pool)
            pool_rest(pool)

        @block.scalar
        def _(act):
            steps = Steps(act, act_s)
            act.wait_ge(cv_in, 32)
            nc.scalar.activation(cvec[:, 2:4, :], cvec[:, 0:2, :], ACT.Sigmoid).then_inc(sig_done, 1)
            act.wait_ge(x_in, 32)
            act.wait_ge(init_done, 1)
            act_stats(act, 0, x4, xn4, 4)
            for q in range(ADA_A):
                act_ada(act, 0, q * NB, q)
            act_high(act, 0, 4, lambda i: mx_hi[:, i:i + 1, :])
            act_split(act, 0, ADA_A)
            for m in range(MIX_M):
                if m + 1 < MIX_M:
                    act_split(act, m + 1, ADA_A + m + 1, min(NB, IN_COLS - (m + 1) * NB))
                act.wait_ge(pe_chunk, 4 * m + 4)
                for b, dst, r, t0 in mix_out(m):
                    if b < 2:
                        if stored(m, b) > 1:
                            act.wait_ge(mix_st[b], 16 * (stored(m, b) - 1))
                        n = TOK - t0
                        nc.scalar.activation(stage[:, b, 0:n], ps[:, mix_bank(m, b), 0:n], ACT.Copy).then_inc(mix_ev_a, 1)
                for b, dst, r, t0 in mix_out(m):
                    act.wait_ge(mix_ev_a if b < 2 else mix_ev_d, evacuated(m, b))
                    act.dma_start(dst, stage[0:r, b, 0:TOK - t0]).then_inc(mix_st[b], 16)
            stage_end(act, 1)
            act.dma_start(at["cos"][:, :, :], a["cos"].rearrange("p (a n) -> p a n", a=4)).then_inc(at_cst, 16)
            act.dma_start(at["sin"][:, :, :], a["sin"].rearrange("p (a n) -> p a n", a=4)).then_inc(at_cst, 16)
            for g, s0, s1 in ((a["k_norm_g"], 0, 4), (a["q_norm_g"], 4, 6)):
                act.dma_start(at["gain"][:, s0:s1, :].rearrange("p s (m d) -> p (s m) d", m=2),
                              g.rearrange("(a o) d -> a o d", o=1).to_broadcast([P, 2 * (s1 - s0), HD])).then_inc(at_cst, 16)
            for i, n in enumerate(("lambda_q1", "lambda_k1", "lambda_q2", "lambda_k2")):
                act.dma_start(at["lq"][:, i, :], a[n].to_broadcast([P, HD])).then_inc(at_cst, 16)
            act.dma_start(at["sub"][:, :], a["subln_g"].rearrange("a p -> p a")).then_inc(at_cst, 16)
            act.wait_ge(at_init, 1)
            nc.scalar.activation(at["lam"][:, 2:4], at["lam"][:, 0:2], ACT.Exp).then_inc(at_lam, 1)
            A = at

            def root_mean_squares(i):
                act.wait_ge(at_ss, i + 1)
                nc.scalar.activation(A["st"][:, 12:24], A["st"][:, 0:12], ACT.Sqrt, scale=1.0 / HD, bias=epsc[:, 0:1]).then_inc(at_std, 1)

            def attend(i, last):
                act.wait_ge(at_tp, i * 2 + 1)
                nc.scalar.activation(A["kT"][:, :], ps[:, 0, :], ACT.Copy).then_inc(at_kT, 1)
                for n in range(4):
                    act.wait_ge(at_mx, i * 4 + (n + 1))
                    nc.scalar.activation(A["e"][:, n, :], ps[:, SC_BANKS[n], :], ACT.Exp, scale=HD ** -0.5,
                                         bias=A["st"][:, 28 + n:29 + n], accum_out=A["st"][:, 32 + n:33 + n]).then_inc(at_e, 1)
                if not last:
                    root_mean_squares(i + 1)
                act_ada_part(act, i + Q_AT)
                act.wait_ge(at_pt, i + 1)
                nc.scalar.activation(A["pT"][:, 0:2, :], ps[:, 0, :].rearrange("p (a t) -> p a t", a=2), ACT.Copy).then_inc(at_pT_a, 1)
                act_ada_store(act, 0, i * NB + Q_AT * NB, i + Q_AT)
                act.wait_ge(at_o, i + 2)
                for t in range(2):
                    steps.inc(nc.scalar.activation(A["junk"][:, t, :], ps[:, 2, t * P:(t + 1) * P], ACT.Square,
                                                   accum_out=A["st"][:, 40 + t:41 + t]))
                steps.wait()
                nc.scalar.activation(A["st"][:, 46:48], A["st"][:, 40:42], ACT.Sqrt, scale=1.0 / P, bias=epsc[:, 0:1]).then_inc(at_std2, 1)

            root_mean_squares(0)
            with act.Fori(0, HEADS - 1) as i:
                steps.enter(i, 2)
                attend(i, False)
            steps.leave(HEADS - 1)
            attend(HEADS - 1, True)
            rwkv_act(act, steps)
            act_rest(act, steps)

        @block.vector
        def _(dve):
            steps = Steps(dve, dve_s)
            steps.inc(nc.vector.memset(s32[:, :, :], 0.0))
            steps.inc(nc.vector.memset(ones[:, :], 1.0))
            steps.inc(nc.vector.memset(epsc[:, 0:1], NORM_EPS))
            steps.inc(nc.vector.memset(epsc[:, 1:2], GN_EPS))
            steps.link(nc.vector.memset(hbuf[:, 0, 0:2 * P], 0.0))
            nc.vector.memset(small[:, :], 0.0).then_inc(init_done, 1)
            dve.wait_ge(sig_done, 1)
            dve.wait_ge(cv_in, 32)
            for i in range(2):
                nc.vector.tensor_tensor(s32[:, :, i], cvec[:, i, :], cvec[:, 2 + i, :], ALU.mult).then_inc(s_ready, 1)
            dve_scale(dve, 0, steps, x4, xn4, 4)
            dve.wait_ge(pt_ps, 1)
            steps.inc(nc.vector.tensor_copy(pcol[:, 0, 0:P0_ROWS], ps[:, 6, 0:P0_ROWS]))
            steps.inc(nc.vector.tensor_copy(pcol[:, 1, 0:P1_ROWS], ps[:, 6, P:P + P1_ROWS]))
            steps.link(nc.vector.tensor_copy(dwc[:, :, :], ps[:, 7, 0:KT * TAPS].rearrange("p (k t) -> p k t", t=TAPS)))
            nc.vector.tensor_copy(small[:, 31:32], small[:, 30:31]).then_inc(pt_ok, 1)
            dve.wait_ge(mt_ps, 1)
            steps.link(nc.vector.tensor_copy(mcol[:, 0:64], ps[:, 6, 0:64]))
            for n, o in ((0, 32), (1, 0)):
                steps.inc(nc.vector.scalar_tensor_tensor(out=gcol[:, n, :], in0=mcol[:, o + 16:o + 32], scalar=1.0,
                                                         in1=col_of("n1g0", 0, KT), op0=ALU.add, op1=ALU.mult))
            steps.wait()
            cols = [(gcol[:, 0, :], mcol[:, 32:48]), (gcol[:, 1, :], mcol[:, 0:16])]
            dve_modulate(dve, 0, 4, cols, lambda i: mx_hi[:, i:i + 1, :], lambda i: mx_lo[:, i:i + 1, :])
            dve_split(dve, 0, ADA_A)
            for m in range(MIX_M):
                if m + 1 < MIX_M:
                    dve_split(dve, m + 1, ADA_A + m + 1, min(NB, IN_COLS - (m + 1) * NB))
                dve.wait_ge(pe_chunk, 4 * m + 4)
                for b, dst, r, t0 in mix_out(m):
                    if b >= 2:
                        if stored(m, b) > 1:
                            dve.wait_ge(mix_st[b], 16 * (stored(m, b) - 1))
                        n = TOK - t0
                        nc.vector.tensor_copy(stage[:, b, 0:n], ps[:, mix_bank(m, b), 0:n]).then_inc(mix_ev_d, 1)
            stage_end(dve, 1)
            A = at
            st = A["st"]
            dve.sem_inc(at_qkr, 2)
            dve.sem_inc(at_o, 1)
            dve.sem_inc(at_y, 1)
            dve.wait_ge(at_cst, 16 * 9)
            steps.inc(nc.vector.tensor_tensor_reduce(out=A["junk"][:, 0, 0:HD], in0=A["lq"][:, 0, :], in1=A["lq"][:, 1, :],
                                                     scale=1.0, scalar=0.0, op0=ALU.mult, op1=ALU.add, accum_out=A["lam"][:, 0:1]))
            steps.inc(nc.vector.tensor_tensor_reduce(out=A["junk"][:, 1, 0:HD], in0=A["lq"][:, 2, :], in1=A["lq"][:, 3, :],
                                                     scale=1.0, scalar=0.0, op0=ALU.mult, op1=ALU.add, accum_out=A["lam"][:, 1:2]))
            steps.wait()
            steps.link(nc.vector.tensor_scalar(A["sub"][:, :], A["sub"][:, :], 1.0 - LAM_INIT, None, ALU.mult))
            nc.vector.memset(A["lam"][:, 6:7], 0.0).then_inc(at_init, 1)
            dve.wait_ge(at_lam, 1)
            steps.link(nc.vector.tensor_tensor(A["lam"][:, 4:5], A["lam"][:, 3:4], A["lam"][:, 2:3], ALU.subtract))
            steps.link(nc.vector.tensor_scalar(A["lam"][:, 5:6], A["lam"][:, 4:5], -LAM_INIT, None, ALU.add))

            def sums_of_squares(i):
                dve.wait_ge(at_qk_in, i * 32 + 32)
                steps.link(nc.vector.tensor_tensor(A["t1"][:, :, :], A["qk"][:, :, :], A["qk"][:, :, :], ALU.mult))
                nc.vector.tensor_reduce(st[:, 0:12], A["t1"][:, :, :].rearrange("p s (m d) -> p (s m) d", m=2), AX_X,
                                        ALU.add).then_inc(at_ss, 1)

            def normalise(i):
                dve.wait_ge(at_std, i + 1)
                steps.link(nc.vector.reciprocal(st[:, 12:24], st[:, 12:24]))
                steps.link(nc.vector.tensor_tensor(A["t2"][:, :, :].rearrange("p s (m d) -> p (s m) d", m=2),
                                                   A["qk"][:, :, :].rearrange("p s (m d) -> p (s m) d", m=2),
                                                   st[:, 12:24].rearrange("p (s a) -> p s a", a=1).to_broadcast([P, 12, HD]), ALU.mult))
                nc.vector.tensor_tensor(A["qkr"][:, 0:2, :], A["t2"][:, 0:2, :], A["gain"][:, 0:2, :], ALU.mult).then_inc(at_qkr, 1)
                steps.link(nc.vector.tensor_tensor(A["t1"][:, 2:6, :], A["t2"][:, 2:6, :], A["gain"][:, 2:6, :], ALU.mult))
                halves = lambda t, h: t.rearrange("p s (x h d) -> p (s x) h d", h=2, d=HD // 4)[:, :, h, :]
                for h in range(2):
                    steps.inc(nc.vector.tensor_tensor(halves(A["t2"][:, 2:6, :], h), halves(A["t1"][:, 2:6, :], 1 - h),
                                                      halves(A["sin"][:, :, :], h), ALU.mult))
                steps.inc(nc.vector.tensor_tensor(A["qkr"][:, 2:6, :], A["t1"][:, 2:6, :], A["cos"][:, :, :], ALU.mult))
                steps.wait()
                nc.vector.tensor_tensor(A["qkr"][:, 2:6, :], A["qkr"][:, 2:6, :], A["t2"][:, 2:6, :], ALU.add).then_inc(at_qkr, 1)

            def attend(i, last):
                dve.wait_ge(at_tp, i * 2 + 2)
                nc.vector.tensor_copy(A["qT"][:, :], ps[:, 1, 0:SEQ]).then_inc(at_qT, 1)
                for n in range(4):
                    dve.wait_ge(at_sc, i * 4 + (n + 1))
                    steps.link(nc.vector.tensor_reduce(st[:, 24 + n:25 + n], ps[:, SC_BANKS[n], :], AX_X, ALU.max))
                    nc.vector.tensor_scalar(st[:, 28 + n:29 + n], st[:, 24 + n:25 + n], -(HD ** -0.5), None, ALU.mult).then_inc(at_mx, 1)
                if not last:
                    sums_of_squares(i + 1)
                dve.wait_ge(at_e, i * 4 + 4)
                steps.link(nc.vector.reciprocal(st[:, 36:40], st[:, 32:36]))
                steps.link(nc.vector.tensor_scalar(st[:, 38:40], st[:, 38:40], A["lam"][:, 5:6], None, ALU.mult))
                for t in range(2):
                    steps.inc(nc.vector.tensor_scalar(A["p"][:, t, :], A["e"][:, t, :], st[:, 36 + t:37 + t], None, ALU.mult))
                steps.wait()
                for t in range(2):
                    nc.vector.scalar_tensor_tensor(out=A["p"][:, t, :], in0=A["e"][:, 2 + t, :], scalar=st[:, 38 + t:39 + t],
                                                   in1=A["p"][:, t, :], op0=ALU.mult, op1=ALU.add).then_inc(at_p, 1)
                dve.wait_ge(at_pt, i + 1)
                nc.vector.tensor_copy(A["pT"][:, 2:4, :], ps[:, 1, :].rearrange("p (a t) -> p a t", a=2)).then_inc(at_pT_d, 1)
                if not last:
                    normalise(i + 1)
                dve.wait_ge(at_std2, i + 1)
                steps.link(nc.vector.reciprocal(st[:, 48:50], st[:, 46:48]))
                for t in range(2):
                    ins = nc.vector.tensor_scalar(A["on"][:, t, :], ps[:, 2, t * P:(t + 1) * P], st[:, 48 + t:49 + t], None, ALU.mult)
                ins.then_inc(at_on, 1)
                dve.wait_ge(at_ot, i + 1)
                nc.vector.tensor_scalar(yT[:, bass.ds(i, 1), :], ps[:, 3:4, 0:SEQ], A["sub"][:, 0:1], None, ALU.mult).then_inc(at_y, 1)

            sums_of_squares(0)
            normalise(0)
            with dve.Fori(0, HEADS - 1) as i:
                steps.enter(i, 16)
                attend(i, False)
            steps.leave(HEADS - 1)
            attend(HEADS - 1, True)
            rwkv_dve(dve, steps)
            dve_rest(dve, steps)

        @block.tensor
        def _(pe):
            pe.wait_ge(cst_in, 32)
            pe.wait_ge(s_ready, 2)
            pe.wait_ge(init_done, 1)
            for q in range(ADA_A):
                for c in range(NCH):
                    pe_ada_chunk(pe, q, q, c)
                pe_ada_sum(pe, q, q % 2, q // 2 + 1)
            pe.wait_ge(prow_in, 16 * 17)
            pe.transpose(ps[:, 6, 0:P0_ROWS], prow[0][0:P0_ROWS, :], ident[0:P0_ROWS, 0:P0_ROWS])
            pe.transpose(ps[:, 6, P:P + P1_ROWS], prow[1][0:P1_ROWS, :], ident[0:P1_ROWS, 0:P1_ROWS])
            for k in range(KT):
                tr = pe.transpose(ps[:, 7, k * TAPS:(k + 1) * TAPS], dwr[:, k * P:(k + 1) * P], ident[0:TAPS, 0:TAPS])
            tr.then_inc(pt_ps, 1)
            pe.wait_ge(mrow_in, 32)
            pe.wait_ge(pt_ok, 1)
            pe.transpose(ps[:, 6, 0:64], mrow[0:64, :], ident[0:64, 0:64]).then_inc(mt_ps, 1)
            pe.wait_ge(norm_xn, 1)
            pe_transposes(pe, 0, xn4, 4)
            for m in range(MIX_M):
                gs = mix_groups(m)
                banks = [b for b, *_ in mix_out(m)]

                def bank_free(g, m=m, banks=banks):
                    if m == 1:
                        pe.wait_ge(tr_ts, 16)
                    elif m > 1:
                        b = banks[g]
                        last = max((n for n in range(m - 2, -1, -2) if any(x[0] == b for x in mix_out(n))), default=None)
                        if last is not None:
                            pe.wait_ge(mix_ev_a if b < 2 else mix_ev_d, evacuated(last, b))

                def activations(c, m=m):
                    if m == 0:
                        pe.wait_ge(tr_hi, 4 * c + 4)
                        pe.wait_ge(tr_lo, 4 * c + 4)

                pe_product(pe, m, gs, activations, bank_free)
            stage_end(pe, 1)
            A = at
            with pe.Fori(0, HEADS) as i:
                pe.wait_ge(at_qkr, i * 2 + 3)
                pe.wait_ge(at_qkr, i * 2 + 4)
                for t in range(4):
                    tr = pe.transpose(ps[:, 0, t * P:(t + 1) * P], A["qkr"][:, t, :], ident[:, :])
                tr.then_inc(at_tp, 1)
                for t in range(2):
                    tr = pe.transpose(ps[:, 1, t * P:(t + 1) * P], A["qkr"][:, 4 + t, :], ident[:, :])
                tr.then_inc(at_tp, 1)
                pe.wait_ge(at_kT, i + 1)
                pe.wait_ge(at_qT, i + 1)
                pe.wait_ge(at_y, i + 1)
                for n, (h, t) in enumerate([(0, 0), (0, 1), (1, 0), (1, 1)]):
                    pe.matmul(ps[:, SC_BANKS[n], :], A["qT"][h * HD:(h + 1) * HD, t * P:(t + 1) * P],
                              A["kT"][h * HD:(h + 1) * HD, :], start=True, stop=True).then_inc(at_sc, 1)
                for c in range(NCH):
                    pe_ada_chunk(pe, i + Q_AT, i + (Q_AT + MIX_M), c)
                for t in range(2):
                    pe.wait_ge(at_p, i * 2 + (t + 1))
                    for k in range(4):
                        tr = pe.transpose(ps[:, k // 2, (k % 2) * SEQ + t * P:(k % 2) * SEQ + (t + 1) * P],
                                          A["p"][:, t, k * P:(k + 1) * P], ident[:, :])
                tr.then_inc(at_pt, 1)
                pe_ada_sum(pe, i + Q_AT, 0, i + (ADA_A // 2 + 1))
                pe.wait_ge(at_pT_a, i + 1)
                pe.wait_ge(at_pT_d, i + 1)
                pe.wait_ge(at_v_in, i * 16 + 16)
                for t in range(2):
                    for k in range(4):
                        mm = pe.matmul(ps[:, 2, t * P:(t + 1) * P], A["pT"][:, k, t * P:(t + 1) * P], A["v"][:, k, :],
                                       start=(k == 0), stop=(k == 3))
                mm.then_inc(at_o, 1)
                pe.wait_ge(at_on, i + 1)
                for t in range(2):
                    tr = pe.transpose(ps[:, 3, t * P:(t + 1) * P], A["on"][:, t, :], ident[:, :])
                tr.then_inc(at_ot, 1)
            rwkv_pe(pe)
            pe_rest(pe)


_INS = ['x', 'c', 'ctx', 'c_ctx', 'ada_w', 'ada_b', 'norm1_g', 'norm2_g', 'mlp_w1', 'mlp_w2', 'mix_in_w', 'mix_out_w',
        'q_norm_g', 'k_norm_g', 'lambda_q1', 'lambda_k1', 'lambda_q2', 'lambda_k2', 'subln_g', 'shift_mu',
        'decay_w0', 'decay_up', 'iclr_a0', 'iclr_up', 'gate_up', 'k_k', 'k_a', 'r_k', 'gn_w', 'gn_b',
        'conv_pw1_w', 'conv_pw1_b', 'conv_dw_w', 'conv_dw_b', 'conv_ln_g', 'conv_ln_b', 'conv_pw2_w', 'conv_pw2_b']


def kernel(**inputs):
    import concourse.bacc as _bacc
    from concourse.bass_utils import run_bass_kernel_spmd as _run

    nc = _bacc.Bacc("TRN2", target_bir_lowering=False, num_devices=1)
    arrays, aps = {}, {}
    for name, v in [(n, inputs[n]) for n in _INS] + list(shape_constants().items()):
        v = np.ascontiguousarray(v)
        arrays[f"in_{name}_dram"] = v
        aps[name] = nc.dram_tensor(f"in_{name}_dram", v.shape, mybir.dt.from_np(v.dtype), kind="ExternalInput").ap()
    out = nc.dram_tensor("out_0_dram", (1, SEQ, D), F32, kind="ExternalOutput").ap()
    build_trunk(nc, aps, out)
    r = _run(nc, [arrays], core_ids=[0])
    return r.results[0]["out_0_dram"]
```
